# Optimizing a Trainium2 kernel written in Bass

```python
import math
import jax, jax.numpy as jnp
from jax import lax
import numpy as np

D_MODEL = 2048
BATCH = 1
SEQ = 512
DEPTH = 1

CHUNK = 64
D_MIX = D_MODEL
ATTN_WIDTH = D_MIX // 2
SSD_WIDTH = D_MIX - ATTN_WIDTH
ATTN_HEAD_DIM = 128
ATTN_Q_HEADS = ATTN_WIDTH // ATTN_HEAD_DIM
ATTN_KV_HEADS = 2
ROPE_THETA = 500000.0
ROPE_PARTIAL_DIV = 4
IDX_HEADS = 16
IDX_HEAD_DIM = 64
IDX_TOPK_MAX = 256
Q_BLOCK = 128
SSD_HEAD_DIM = 64
SSD_HEADS = SSD_WIDTH // SSD_HEAD_DIM
SSD_GROUPS = 4
SSD_HEADS_PER_GROUP = SSD_HEADS // SSD_GROUPS
SSD_STATE = 128
SSD_CONV = 4
SSD_CHUNK = CHUNK
SSD_XBC_WIDTH = SSD_WIDTH + 2 * SSD_GROUPS * SSD_STATE
DEEPNORM_ALPHA = (2.0 * DEPTH) ** 0.25
DEEPNORM_BETA = (8.0 * DEPTH) ** -0.25
LN_EPS = 1e-5
RMS_EPS = 1e-5
IN_WIDTHS = (
    ATTN_Q_HEADS * ATTN_HEAD_DIM,
    ATTN_KV_HEADS * ATTN_HEAD_DIM,
    ATTN_KV_HEADS * ATTN_HEAD_DIM,
    ATTN_WIDTH,
    IDX_HEADS * IDX_HEAD_DIM,
    IDX_HEAD_DIM,
    IDX_HEADS,
    SSD_WIDTH,
    SSD_XBC_WIDTH,
    SSD_HEADS,
)
IN_TOTAL = sum(IN_WIDTHS)
VALUE_COL = 2


def _split_cols(u, widths):
    out, start = [], 0
    for w in widths:
        out.append(u[..., start:start + w])
        start += w
    return out

def _layer_norm(x, g, b):
    x32 = x.astype(jnp.float32)
    mu = jnp.mean(x32, axis=-1, keepdims=True)
    var = jnp.mean(jnp.square(x32 - mu), axis=-1, keepdims=True)
    y = (x32 - mu) * lax.rsqrt(var + LN_EPS) * g.astype(jnp.float32) + b.astype(jnp.float32)
    return y.astype(x.dtype)

def _rope_partial(t, pos):
    d = t.shape[-1]
    rot = d // ROPE_PARTIAL_DIV
    half = rot // 2
    inv = ROPE_THETA ** (-jnp.arange(half, dtype=jnp.float32) * 2.0 / rot)
    ang = pos[:, None] * inv[None, :]
    cos = jnp.cos(ang)[:, None, :]
    sin = jnp.sin(ang)[:, None, :]
    t32 = t.astype(jnp.float32)
    x1 = t32[..., :half]
    x2 = t32[..., half:rot]
    out = jnp.concatenate([x1 * cos - x2 * sin, x2 * cos + x1 * sin, t32[..., rot:]], axis=-1)
    return out.astype(t.dtype)

def _dsa_attention(q, k, v, q_idx, k_idx, w_idx):
    bsz, seq = q.shape[0], q.shape[1]
    topk = min(IDX_TOPK_MAX, seq // 4)
    rep = ATTN_Q_HEADS // ATTN_KV_HEADS
    scale = ATTN_HEAD_DIM ** -0.5
    key_chunk = jnp.arange(seq) // CHUNK
    k_idx32 = k_idx.astype(jnp.float32)
    gather = jax.vmap(lambda a, ix: a[ix])

    def block(i):
        start = i * Q_BLOCK
        sl = lambda a: lax.dynamic_slice_in_dim(a, start, Q_BLOCK, axis=1)
        qb, qib, wb = sl(q), sl(q_idx), sl(w_idx)
        q_chunk = (start + jnp.arange(Q_BLOCK)) // CHUNK
        logits = jax.nn.relu(jnp.einsum('bqhd,bsd->bqhs', qib.astype(jnp.float32), k_idx32))
        score = jnp.einsum('bqhs,bqh->bqs', logits, wb.astype(jnp.float32))
        admissible = key_chunk[None, :] <= q_chunk[:, None]
        score = jnp.where(admissible[None], score, -jnp.inf)
        _, sel = lax.top_k(score, topk)
        valid = key_chunk[sel] <= q_chunk[None, :, None]
        kg = gather(k, sel)
        vg = gather(v, sel)
        qg = qb.reshape(bsz, Q_BLOCK, ATTN_KV_HEADS, rep, ATTN_HEAD_DIM)
        s = jnp.einsum('bqgrd,bqkgd->bqgrk', qg, kg).astype(jnp.float32) * scale
        s = jnp.where(valid[:, :, None, None, :], s, -jnp.inf)
        p = jax.nn.softmax(s, axis=-1).astype(vg.dtype)
        o = jnp.einsum('bqgrk,bqkgd->bqgrd', p, vg)
        return o.reshape(bsz, Q_BLOCK, ATTN_Q_HEADS * ATTN_HEAD_DIM)

    out = lax.map(block, jnp.arange(seq // Q_BLOCK))
    return out.transpose(1, 0, 2, 3).reshape(bsz, seq, ATTN_Q_HEADS * ATTN_HEAD_DIM)

def _causal_depthwise_conv(u, w, b):
    c = u.shape[-1]
    y = lax.conv_general_dilated(u, w[:, None, :], window_strides=(1,), padding=[(SSD_CONV - 1, 0)],
                                 dimension_numbers=('NWC', 'WIO', 'NWC'), feature_group_count=c)
    return y + b

def _ssd_mixer(xbc, z, dt_raw, conv_w, conv_b, dt_bias, a_log, d_skip, norm_w):
    bsz, seq, _ = xbc.shape
    G, R, P, N, l = SSD_GROUPS, SSD_HEADS_PER_GROUP, SSD_HEAD_DIM, SSD_STATE, SSD_CHUNK
    nc = seq // l
    xbc = jax.nn.silu(_causal_depthwise_conv(xbc, conv_w, conv_b))
    xs, bm, cm = _split_cols(xbc, (SSD_WIDTH, G * N, G * N))
    xs = xs.astype(jnp.float32).reshape(bsz, nc, l, G, R, P)
    bm = bm.astype(jnp.float32).reshape(bsz, nc, l, G, N)
    cm = cm.astype(jnp.float32).reshape(bsz, nc, l, G, N)
    dt = jax.nn.softplus(dt_raw.astype(jnp.float32) + dt_bias.astype(jnp.float32))
    dt = dt.reshape(bsz, nc, l, G, R)
    a = -jnp.exp(a_log.astype(jnp.float32)).reshape(G, R)
    xdt = xs * dt[..., None]
    a_cum = jnp.cumsum(dt * a, axis=2)
    seg = a_cum[:, :, :, None] - a_cum[:, :, None, :]
    tril = jnp.tril(jnp.ones((l, l), dtype=bool))[:, :, None, None]
    lmat = jnp.exp(jnp.where(tril, seg, -jnp.inf))
    cb = jnp.einsum('bclgn,bcsgn->bclsg', cm, bm)
    y_diag = jnp.einsum('bclsg,bclsgr,bcsgrp->bclgrp', cb, lmat, xdt)
    decay = jnp.exp(a_cum[:, :, -1:] - a_cum)
    states = jnp.einsum('bcsgn,bcsgr,bcsgrp->bcgrpn', bm, decay, xdt)
    chunk_decay = jnp.exp(a_cum[:, :, -1])

    def step(h, inp):
        st, dec = inp
        return h * dec[..., None, None] + st, h

    h0 = jnp.zeros((bsz, G, R, P, N), jnp.float32)
    _, prev = lax.scan(step, h0, (jnp.moveaxis(states, 1, 0), jnp.moveaxis(chunk_decay, 1, 0)))
    prev = jnp.moveaxis(prev, 0, 1)
    y_off = jnp.einsum('bclgn,bcgrpn,bclgr->bclgrp', cm, prev, jnp.exp(a_cum))
    y = y_diag + y_off + d_skip.astype(jnp.float32).reshape(G, R)[:, :, None] * xs
    y = y.reshape(bsz, seq, SSD_WIDTH)
    g = (y * jax.nn.silu(z.astype(jnp.float32))).reshape(bsz, seq, G, SSD_WIDTH // G)
    g = g * lax.rsqrt(jnp.mean(jnp.square(g), axis=-1, keepdims=True) + RMS_EPS)
    return (g.reshape(bsz, seq, SSD_WIDTH) * norm_w.astype(jnp.float32)).astype(z.dtype)

def first_inputs(seed: int = 0) -> dict:
    key = jax.random.key(seed)
    ks = jax.random.split(key, 12)
    x = jax.random.normal(ks[0], (BATCH, SEQ, D_MODEL), jnp.float32)
    blk_keys = jax.random.split(ks[1], len(IN_WIDTHS))
    blocks = []
    for j, w in enumerate(IN_WIDTHS):
        scale = D_MODEL ** -0.5 * (DEEPNORM_BETA if j == VALUE_COL else 1.0)
        blocks.append(jax.random.normal(blk_keys[j], (DEPTH, D_MODEL, w), jnp.float32) * scale)
    w_in = jnp.concatenate(blocks, axis=-1)
    w_out = jax.random.normal(ks[2], (DEPTH, D_MIX, D_MODEL), jnp.float32) * (D_MIX ** -0.5 * DEEPNORM_BETA)
    conv_w = jax.random.normal(ks[3], (DEPTH, SSD_CONV, SSD_XBC_WIDTH), jnp.float32) * SSD_CONV ** -0.5
    conv_b = 0.01 * jax.random.normal(ks[4], (DEPTH, SSD_XBC_WIDTH), jnp.float32)
    u = jax.random.uniform(ks[5], (DEPTH, SSD_HEADS), jnp.float32)
    dt0 = jnp.exp(u * (math.log(0.1) - math.log(0.001)) + math.log(0.001))
    dt_bias = dt0 + jnp.log(-jnp.expm1(-dt0))
    a_log = jnp.log(jax.random.uniform(ks[6], (DEPTH, SSD_HEADS), jnp.float32, 1.0, 16.0))
    d_skip = 1.0 + 0.1 * jax.random.normal(ks[7], (DEPTH, SSD_HEADS), jnp.float32)
    ssd_norm_w = 1.0 + 0.1 * jax.random.normal(ks[8], (DEPTH, SSD_WIDTH), jnp.float32)
    ln_g = 1.0 + 0.1 * jax.random.normal(ks[9], (DEPTH, D_MODEL), jnp.float32)
    ln_b = 0.01 * jax.random.normal(ks[10], (DEPTH, D_MODEL), jnp.float32)
    return {"x": x, "w_in": w_in, "w_out": w_out, "conv_w": conv_w, "conv_b": conv_b,
            "dt_bias": dt_bias, "a_log": a_log, "d_skip": d_skip, "ssd_norm_w": ssd_norm_w,
            "ln_g": ln_g, "ln_b": ln_b}

def first_block(x, w_in, w_out, conv_w, conv_b, dt_bias, a_log, d_skip, ssd_norm_w, ln_g, ln_b):
    bsz, seq, _ = x.shape
    pos = jnp.arange(seq, dtype=jnp.float32)
    h = x
    for layer in range(DEPTH):
        u = jnp.einsum('bsd,de->bse', h, w_in[layer])
        q, k, v, z_attn, q_idx, k_idx, w_idx, z_ssd, xbc, dt_raw = _split_cols(u, IN_WIDTHS)
        q = _rope_partial(q.reshape(bsz, seq, ATTN_Q_HEADS, ATTN_HEAD_DIM), pos)
        k = _rope_partial(k.reshape(bsz, seq, ATTN_KV_HEADS, ATTN_HEAD_DIM), pos)
        v = v.reshape(bsz, seq, ATTN_KV_HEADS, ATTN_HEAD_DIM)
        q_idx = _rope_partial(q_idx.reshape(bsz, seq, IDX_HEADS, IDX_HEAD_DIM), pos)
        k_idx = _rope_partial(k_idx[:, :, None, :], pos)[:, :, 0, :]
        w_idx = w_idx * (IDX_HEADS ** -0.5 * IDX_HEAD_DIM ** -0.5)
        o_attn = _dsa_attention(q, k, v, q_idx, k_idx, w_idx) * jax.nn.silu(z_attn)
        o_ssd = _ssd_mixer(xbc, z_ssd, dt_raw, conv_w[layer], conv_b[layer], dt_bias[layer],
                           a_log[layer], d_skip[layer], ssd_norm_w[layer])
        mixed = jnp.concatenate([o_attn, o_ssd.astype(o_attn.dtype)], axis=-1)
        sub = jnp.einsum('bse,ed->bsd', mixed, w_out[layer])
        h = _layer_norm(DEEPNORM_ALPHA * h + sub, ln_g[layer], ln_b[layer])
    return h


GROUP_WIDTH = 128
HEAD_DIM = 128
D_GMLP = D_MODEL // 4
D_SB = D_MODEL // 4
D_MIX_2 = D_GMLP + D_SB
N_GMLP_GROUPS = D_GMLP // GROUP_WIDTH
N_SB_HEADS = D_SB // HEAD_DIM
N_MIX_GROUPS = D_MIX_2 // GROUP_WIDTH
D_IN = 2 * D_GMLP + 3 * D_SB
SPLIT_POINTS = (D_GMLP, 2 * D_GMLP, 2 * D_GMLP + D_SB, 2 * D_GMLP + 2 * D_SB)
CHUNK_2 = 128
N_GROUPS = 4
EXPERTS_PER_GROUP = 8
N_EXPERTS = N_GROUPS * EXPERTS_PER_GROUP
TOP_K = 2
D_EXPERT = D_MODEL // 8
EXPERT_BLOCK = 128
N_MOD = 6
EPS = 1e-6


def rms_norm(x, g):
    xf = x.astype(jnp.float32)
    y = xf * lax.rsqrt(jnp.mean(xf * xf, axis=-1, keepdims=True) + EPS)
    return (y * g.astype(jnp.float32)).astype(x.dtype)

def chunked_spatial_gating(u, v, norm_g, ws, bs):
    B, S, _ = u.shape
    u = jax.nn.gelu(u, approximate=False)
    v = jax.nn.gelu(v, approximate=False).reshape(B, S // CHUNK_2, CHUNK_2, N_GMLP_GROUPS, GROUP_WIDTH)
    v = rms_norm(v, norm_g.reshape(N_GMLP_GROUPS, GROUP_WIDTH))
    w = ws * jnp.tril(jnp.ones((CHUNK_2, CHUNK_2), ws.dtype))
    s = jnp.einsum('gtp,bcpgk->bctgk', w, v) + bs.T[:, :, None]
    return u * s.reshape(B, S, D_GMLP)

def stick_breaking_attention(q, k, v):
    B, S, H, dh = q.shape
    nq = S // Q_BLOCK
    scale = HEAD_DIM ** -0.5
    qf = q.astype(jnp.float32).transpose(0, 2, 1, 3)
    kf = k.astype(jnp.float32).transpose(0, 2, 1, 3)
    vt = v.transpose(0, 2, 1, 3)
    idx = jnp.arange(Q_BLOCK, dtype=jnp.int32)
    after_in_block = (idx[:, None] > idx[None, :]).astype(jnp.float32)
    outs = []
    for n in range(nq):
        nk = n + 1
        kl = nk * Q_BLOCK
        qb = qf[:, :, n * Q_BLOCK:kl]
        z = jnp.einsum('bhqd,bhkd->bhqk', qb, kf[:, :, :kl]) * scale
        q_pos = n * Q_BLOCK + idx
        causal = jnp.arange(kl, dtype=jnp.int32)[None, :] < q_pos[:, None]
        log_fail = jnp.where(causal, jax.nn.log_sigmoid(-z), 0.0).reshape(B, H, Q_BLOCK, nk, Q_BLOCK)
        within = jnp.einsum('bhqni,ij->bhqnj', log_fail, after_in_block)
        blk = jnp.sum(log_fail, axis=-1)
        later = lax.cumsum(blk, axis=3, reverse=True) - blk
        log_a = jax.nn.log_sigmoid(z) + (within + later[..., None]).reshape(B, H, Q_BLOCK, kl)
        a = jnp.where(causal, jnp.exp(log_a), 0.0)
        outs.append(jnp.einsum('bhqk,bhkd->bhqd', a.astype(vt.dtype), vt[:, :, :kl]))
    o = jnp.concatenate(outs, axis=2)
    return o.transpose(0, 2, 1, 3).reshape(B, S, H * dh)

def hierarchical_moe(h, w_group, b_group, w_route, b_route, w_gate, w_up, w_down):
    n, d = h.shape
    hf = h.astype(jnp.float32)
    g_logits = hf @ w_group.astype(jnp.float32) + b_group.astype(jnp.float32)
    g_prob = jax.nn.softmax(g_logits, axis=-1)
    g_idx = jnp.argmax(g_logits, axis=-1).astype(jnp.int32)
    p_group = jnp.take_along_axis(g_prob, g_idx[:, None], axis=-1)
    e_logits = (hf @ w_route.astype(jnp.float32) + b_route.astype(jnp.float32)).reshape(n, N_GROUPS, EXPERTS_PER_GROUP)
    e_logits = jnp.take_along_axis(e_logits, g_idx[:, None, None], axis=1)[:, 0]
    top_val, top_idx = lax.top_k(e_logits, TOP_K)
    weights = jax.nn.softmax(top_val, axis=-1) * p_group
    expert_id = g_idx[:, None] * EXPERTS_PER_GROUP + top_idx.astype(jnp.int32)

    a = n * TOP_K
    flat_e = expert_id.reshape(a)
    flat_tok = jnp.repeat(jnp.arange(n, dtype=jnp.int32), TOP_K)
    order = jnp.argsort(flat_e)
    sorted_e = flat_e[order]
    counts = jnp.bincount(flat_e, length=N_EXPERTS).astype(jnp.int32)
    start = jnp.cumsum(counts) - counts
    padded = (counts + EXPERT_BLOCK - 1) // EXPERT_BLOCK * EXPERT_BLOCK
    pend = jnp.cumsum(padded)
    pstart = pend - padded
    rank = jnp.arange(a, dtype=jnp.int32) - start[sorted_e]
    slot = jnp.zeros((a,), jnp.int32).at[order].set((pstart[sorted_e] + rank).astype(jnp.int32))
    n_blocks = (a + EXPERT_BLOCK - 1) // EXPERT_BLOCK + N_EXPERTS
    capacity = n_blocks * EXPERT_BLOCK
    slot_tok = jnp.full((capacity,), n, jnp.int32).at[slot].set(flat_tok)
    block_e = jnp.minimum(
        jnp.searchsorted(pend, jnp.arange(n_blocks, dtype=jnp.int32) * EXPERT_BLOCK, side='right'),
        N_EXPERTS - 1).astype(jnp.int32)
    h_pad = jnp.concatenate([h, jnp.zeros((1, d), h.dtype)], axis=0)
    xs = h_pad[slot_tok].reshape(n_blocks, EXPERT_BLOCK, d)

    def expert_block(args):
        xb, e = args
        act = jax.nn.silu(xb @ w_gate[e]) * (xb @ w_up[e])
        return act @ w_down[e]

    ys = lax.map(expert_block, (xs, block_e)).reshape(capacity, d)
    picked = ys[slot].reshape(n, TOP_K, d)
    return jnp.einsum('nkd,nk->nd', picked, weights.astype(picked.dtype))

def second_inputs(seed: int = 0) -> dict:
    key = jax.random.key(seed)
    ks = jax.random.split(key, 22)
    f32 = jnp.float32
    L, D = DEPTH, D_MODEL

    def nrm(k, shape, s):
        return jax.random.normal(k, shape, f32) * s

    return {
        "x": nrm(ks[0], (BATCH, SEQ, D), 1.0),
        "c": nrm(ks[1], (BATCH, D), 1.0),
        "w_mod": nrm(ks[2], (D, N_MOD * D), 0.5 * D ** -0.5),
        "b_mod": nrm(ks[3], (N_MOD * D,), 0.02),
        "mod_layer": nrm(ks[4], (L, N_MOD * D), 0.1),
        "norm1_g": 1.0 + nrm(ks[5], (L, D), 0.02),
        "w_in": nrm(ks[6], (L, D, D_IN), D ** -0.5),
        "gm_norm_g": 1.0 + nrm(ks[7], (L, D_GMLP), 0.02),
        "gm_ws": nrm(ks[8], (L, N_GMLP_GROUPS, CHUNK_2, CHUNK_2), CHUNK_2 ** -0.5),
        "gm_bs": 1.0 + nrm(ks[9], (L, N_GMLP_GROUPS, CHUNK_2), 0.1),
        "q_norm_g": 1.0 + nrm(ks[10], (L, HEAD_DIM), 0.02),
        "k_norm_g": 1.0 + nrm(ks[11], (L, HEAD_DIM), 0.02),
        "out_norm_g": 1.0 + nrm(ks[12], (L, D_MIX_2), 0.02),
        "w_out": nrm(ks[13], (L, D_MIX_2, D), D_MIX_2 ** -0.5),
        "norm2_g": 1.0 + nrm(ks[14], (L, D), 0.02),
        "w_group": nrm(ks[15], (L, D, N_GROUPS), D ** -0.5),
        "b_group": nrm(ks[16], (L, N_GROUPS), 0.01),
        "w_route": nrm(ks[17], (L, D, N_EXPERTS), D ** -0.5),
        "b_route": nrm(ks[18], (L, N_EXPERTS), 0.01),
        "w_gate": nrm(ks[19], (L, N_EXPERTS, D, D_EXPERT), D ** -0.5),
        "w_up": nrm(ks[20], (L, N_EXPERTS, D, D_EXPERT), D ** -0.5),
        "w_down": nrm(ks[21], (L, N_EXPERTS, D_EXPERT, D), D_EXPERT ** -0.5),
    }

def second_block(x, c, w_mod, b_mod, mod_layer, norm1_g, w_in, gm_norm_g, gm_ws, gm_bs,
              q_norm_g, k_norm_g, out_norm_g, w_out, norm2_g, w_group, b_group,
              w_route, b_route, w_gate, w_up, w_down):
    B, S, D = x.shape
    mod_shared = jax.nn.silu(c) @ w_mod + b_mod
    for l in range(DEPTH):
        mod = (mod_shared + mod_layer[l])[:, None, :]
        shift1, scale1, gate1, shift2, scale2, gate2 = jnp.split(mod, N_MOD, axis=-1)

        h = rms_norm(x, norm1_g[l]) * (1.0 + scale1) + shift1
        proj = h @ w_in[l]
        u_a, v_a, q, k, v = jnp.split(proj, SPLIT_POINTS, axis=-1)
        y_a = chunked_spatial_gating(u_a, v_a, gm_norm_g[l], gm_ws[l], gm_bs[l])
        q = rms_norm(q.reshape(B, S, N_SB_HEADS, HEAD_DIM), q_norm_g[l])
        k = rms_norm(k.reshape(B, S, N_SB_HEADS, HEAD_DIM), k_norm_g[l])
        v = v.reshape(B, S, N_SB_HEADS, HEAD_DIM)
        y_b = stick_breaking_attention(q, k, v)
        y = jnp.concatenate([y_a, y_b], axis=-1).reshape(B, S, N_MIX_GROUPS, GROUP_WIDTH)
        y = rms_norm(y, out_norm_g[l].reshape(N_MIX_GROUPS, GROUP_WIDTH)).reshape(B, S, D_MIX_2)
        x = x + gate1 * (y @ w_out[l])

        h = rms_norm(x, norm2_g[l]) * (1.0 + scale2) + shift2
        m = hierarchical_moe(h.reshape(B * S, D), w_group[l], b_group[l], w_route[l], b_route[l],
                             w_gate[l], w_up[l], w_down[l]).reshape(B, S, D)
        x = x + gate2 * m
    return x


def setup_inputs(seed=0):
    out = dict(first_inputs(seed))
    for name, value in second_inputs(seed + 1).items():
        if name != "x":
            out[name + "_2"] = value
    return out


def reference(
    x, w_in, w_out, conv_w, conv_b, dt_bias, a_log, d_skip, ssd_norm_w, ln_g, ln_b, c_2,
    w_mod_2, b_mod_2, mod_layer_2, norm1_g_2, w_in_2, gm_norm_g_2, gm_ws_2, gm_bs_2, q_norm_g_2,
    k_norm_g_2, out_norm_g_2, w_out_2, norm2_g_2, w_group_2, b_group_2, w_route_2, b_route_2,
    w_gate_2, w_up_2, w_down_2,
):
    x = first_block(
        x, w_in, w_out, conv_w, conv_b, dt_bias, a_log, d_skip, ssd_norm_w, ln_g, ln_b,
    )
    return second_block(
        x, c_2, w_mod_2, b_mod_2, mod_layer_2, norm1_g_2, w_in_2, gm_norm_g_2, gm_ws_2, gm_bs_2,
        q_norm_g_2, k_norm_g_2, out_norm_g_2, w_out_2, norm2_g_2, w_group_2, b_group_2,
        w_route_2, b_route_2, w_gate_2, w_up_2, w_down_2,
    )


_drawn_inputs = setup_inputs


def setup_inputs(seed=0):
    import zlib

    import numpy as np

    out = dict(_drawn_inputs(seed))
    spreads = {}
    factors = {'conv_b': 7.585,
     'ln_b': 3.834,
     'norm1_g_2': 5.291,
     'gm_norm_g_2': 8.0,
     'gm_bs_2': 4.269,
     'q_norm_g_2': 8.0,
     'k_norm_g_2': 8.0,
     'out_norm_g_2': 6.091,
     'norm2_g_2': 4.954,
     'b_group_2': 8.0,
     'b_route_2': 8.0}
    for name, (base, spread) in spreads.items():
        noise = np.random.default_rng([zlib.crc32(name.encode()), seed]).standard_normal(out[name].shape)
        drawn = base * np.exp(spread * noise) if base else spread * noise
        out[name] = __import__('jax').numpy.asarray(drawn.astype(out[name].dtype))
    for name, factor in factors.items():
        out[name] = (out[name] * factor).astype(out[name].dtype)
    return out
```

```python
import concourse.bass as bass
from concourse import mybir
from contextlib import ExitStack
import numpy as np

F32 = mybir.dt.float32
I32 = mybir.dt.int32
ALU = mybir.AluOpType
ACT = mybir.ActivationFunctionType
AX = mybir.AxisListType

P = 128
S = 512
D = 2048
TT = S // P
KD = D // P
BLK = 64
NE, NG, EPG, DE = 32, 4, 8, 256
NBLK = 48
QH, KVH, DH = 8, 2, 128
IH, ID = 16, 64
TOPK = 128
SG, SR, SP_ = 4, 4, 64
ALPHA = 2.0 ** 0.25
NEG = -1e30
OUT_OF_REACH = -3.3e38
TAKEN = -3.4e38

C_Q, C_K, C_ZA, C_QI, C_KI, C_Z, C_XBC, C_DT = 0, 1024, 1536, 2560, 3584, 3664, 4688, 6736


def host_constants():
    p = np.arange(P)[:, None]
    f = np.arange(P)[None, :]
    tok = (np.arange(TT)[None, :] * P + p).astype(np.float32)

    def rope(rot, theta=500000.0):
        half = rot // 2
        inv = np.float32(theta) ** (-np.arange(half, dtype=np.float32) * np.float32(2.0) / np.float32(rot))
        ang = (tok[:, :, None] * inv.astype(np.float32)[None, None, :]).astype(np.float32)
        c, s = np.cos(ang.astype(np.float64)), np.sin(ang.astype(np.float64))
        return (np.concatenate([c, c], -1).reshape(P, -1), np.concatenate([s, -s], -1).reshape(P, -1))

    cos_a, sin_a = rope(DH // 4)
    cos_i, sin_i = rope(ID // 4)
    parts = {
        "ident": (p == f),
        "upto": (p <= f),
        "before": (p < f),
        "not_before": np.where(p >= f, NEG, 0.0),
        "neg_from": -(p >= f).astype(np.float32),
        "neg_ones": -np.ones((P, P)),
        "ones": np.ones((P, P)),
        "late_chunk": ((p < 64) & (f >= 64)),
        "cos_a": cos_a, "sin_a": sin_a, "cos_i": cos_i, "sin_i": sin_i,
        "thresholds": np.broadcast_to((np.arange(8) * BLK).astype(np.float32)[None, :], (P, 8)),
        "block_no": np.broadcast_to(np.arange(NBLK, dtype=np.float32)[None, :], (P, NBLK)),
        "rank4": np.broadcast_to((4.0 - np.arange(4))[None, :], (P, 4)),
        "rank8": np.broadcast_to((8.0 - np.arange(8))[None, :], (P, 8)),
        "tokens": tok,
    }
    at, cols, out = 0, {}, []
    for name, a in parts.items():
        a = np.ascontiguousarray(a).astype(np.float32)
        cols[name] = (at, at + a.shape[1])
        at += a.shape[1]
        out.append(a)
    return np.concatenate(out, 1), cols


CONST, COLS = host_constants()


class Steps:

    def __init__(self, eng, own):
        self.eng, self.own, self.n, self.last, self.counts = eng, own, 0, None, {}

    def do(self, ins, sem=None, value=None):
        if sem is None:
            self.n += 1
            ins.then_inc(self.own, 1)
            self.last = (self.own, self.n)
        else:
            if value is None:
                value = self.counts[sem.name] = self.counts.get(sem.name, 0) + 1
            ins.then_inc(sem, 1)
            self.last = (sem, value)

    def settle(self):
        self.eng.wait_ge(*self.last)


def program(nc, a, out):
    ctx = ExitStack()
    with ctx:
        def sb(name, shape, dt=F32):
            return ctx.enter_context(nc.sbuf_tensor(name, shape, dt))

        sems = {}

        def sem(name):
            if name not in sems:
                sems[name] = ctx.enter_context(nc.semaphore(name))
            return sems[name]

        RX = sb("RX", [P, 8192])
        RH = sb("RH", [P, 8192])
        RM = sb("RM", [P, 8192])
        RW = sb("RW", [P, 8192])
        RA = sb("RA", [P, 10240])
        RG = sb("RG", [P, 6144])
        cst = sb("cst", [P, CONST.shape[1]])
        C = {k: cst[:, i:j] for k, (i, j) in COLS.items()}
        ident = C["ident"]
        ps = [ctx.enter_context(nc.psum_tensor(f"bank{i}", [P, 512], F32)) for i in range(8)]

        X = RX[:, :].rearrange("p (k t) -> p k t", k=KD)
        H = RH[:, :].rearrange("p (t d) -> p t d", t=TT)
        Hx = RH[:, :].rearrange("p (t q k) -> p t k q", t=TT, k=KD)
        M = RM[:, :].rearrange("p (k t) -> p k t", k=KD)
        W = RW[:, :].rearrange("p (s k n) -> p s k n", s=4, k=4)
        macc = RG[:, 0:2048]
        mring = RG[:, 2048:6144].rearrange("p (s n) -> p s n", s=2)
        xs = RH[:, 0:4096].rearrange("p (t e) -> p t e", t=TT)
        bfm = RH[:, 4096:6144].rearrange("p (g t) -> p g t", g=SG)
        cfm = RH[:, 6144:8192].rearrange("p (g t) -> p g t", g=SG)
        btm = RA[:, 0:2048].rearrange("p (t e) -> p t e", t=TT)
        SL = RA[:, 2048:4096].rearrange("p (s t) -> p s t", s=4)
        CV = RA[:, 4096:5120].rearrange("p (s t) -> p s t", s=2)
        xdt = RA[:, 2048:4096].rearrange("p (s e) -> p s e", s=2)
        xdd = RA[:, 4096:6144].rearrange("p (s e) -> p s e", s=2)
        Hst = RA[:, 6144:7168]
        Dm = RA[:, 7168:8192].rearrange("p (s r l) -> p s r l", s=2, r=SR)
        Mt = RA[:, 8192:9216].rearrange("p (s r l) -> p s r l", s=2, r=SR)
        GT = RA[:, 9216:9472].rearrange("p (s l) -> p s l", s=2)
        t1 = RA[:, 9472:9728]
        t2 = RA[:, 9728:9984]
        Z = RM[:, 0:4096].rearrange("p (t e) -> p t e", t=TT)
        qT = RH[:, 0:4096].rearrange("p (h t) -> p h t", h=QH)
        qiT = RH[:, 4096:8192].rearrange("p (h t) -> p h t", h=QH)
        kT = RA[:, 0:1024].rearrange("p (h t) -> p h t", h=KVH)
        kiT = sb("kiT", [P, S])[:, :]
        V = RA[:, 1536:2560].rearrange("p (t e) -> p t e", t=TT)
        SC = RA[:, 2560:3072]
        BIAS = RA[:, 3072:3584]
        R = RA[:, 3584:4608].rearrange("p (s n) -> p s n", s=2)
        Pb = RA[:, 4608:6656].rearrange("p (h n) -> p h n", h=4)
        T = RA[:, 4608:6656].rearrange("p (t n) -> p t n", t=TT)
        PT = RA[:, 6656:8704].rearrange("p (k n) -> p k n", k=4)
        RT = RA[:, 6656:7680].rearrange("p (s n) -> p s n", s=2)
        TK = RA[:, 8704:9216].rearrange("p (t n) -> p t n", t=TT)
        lng = RA[:, 0:2048]
        lnb = RA[:, 2048:4096]
        junk = RA[:, 4096:6144]
        XN = RM[:, :].rearrange("p (t d) -> p t d", t=TT)
        XNx = RM[:, :].rearrange("p (t q k) -> p t k q", t=TT, k=KD)
        VA = RA[:, 0:2048].rearrange("p (t e) -> p t e", t=TT)
        UA = RA[:, 2048:4096].rearrange("p (t e) -> p t e", t=TT)
        T2 = RA[:, 4096:6144].rearrange("p (t e) -> p t e", t=TT)
        V2 = RA[:, 6144:8192].rearrange("p (t e) -> p t e", t=TT)
        SQ = RA[:, 8192:10240].rearrange("p (t e) -> p t e", t=TT)
        qT2 = RM[:, 0:2048].rearrange("p (h t) -> p h t", h=4)
        kT2 = RM[:, 2048:4096].rearrange("p (h t) -> p h t", h=4)
        Y = RM[:, 4096:8192].rearrange("p (t e) -> p t e", t=TT)
        yT = RX[:, 0:4096].rearrange("p (k t) -> p k t", k=8)
        off = [0, 512, 896, 1152]
        SPl = [RX[:, 4096 + off[j]:4096 + off[j] + S - P * j] for j in range(4)]
        AT = [RX[:, 5376 + off[j]:5376 + off[j] + S - P * j] for j in range(4)]
        EA = RX[:, 6656:7680].rearrange("p (s n) -> p s n", s=2)
        YSQ = RX[:, 4096:8192].rearrange("p (t e) -> p t e", t=TT)
        gate = RA[:, 0:2048]
        gtmp = RA[:, 2048:2560]
        WGt = [RX[:, 4096 * u:4096 * (u + 1)].rearrange("p (k n) -> p k n", k=KD) for u in range(2)]
        WUt = [RM[:, 4096 * u:4096 * (u + 1)].rearrange("p (k n) -> p k n", k=KD) for u in range(2)]
        WDt = [RW[:, 4096 * u:4096 * (u + 1)].rearrange("p (m n) -> p m n", m=2) for u in range(2)]
        xg = [RG[0:BLK, 2048 * u:2048 * (u + 1)] for u in range(2)]
        xgx = [RG[0:BLK, 2048 * u:2048 * (u + 1)].rearrange("p (q k) -> p k q", k=KD) for u in range(2)]
        xgT = [RG[:, 4096 + 1024 * u:4096 + 1024 * (u + 1)].rearrange("p (k s) -> p k s", k=KD) for u in range(2)]
        yb = [RA[0:BLK, 2048 * u:2048 * (u + 1)] for u in range(2)]
        xmul = RA[:, 4096:5120].rearrange("p (k s) -> p k s", k=KD)
        SGt = [RA[:, 5120 + 128 * u:5248 + 128 * u] for u in range(2)]
        hb = [RA[:, 5376 + 128 * u:5504 + 128 * u].rearrange("p (m s) -> p m s", m=2) for u in range(2)]
        picked = [[RX[:, 4096 * u + 2048 * k:4096 * u + 2048 * (k + 1)] for k in range(2)] for u in range(2)]

        SM = sb("SM", [P, TT, 96])
        dtb = sb("dtb", [P, 16])
        alog = sb("alog", [P, 16])
        dsk = sb("dsk", [P, 16])
        convw = sb("convw", [P, 64])
        packrow = sb("packrow", [108, P])
        pack = sb("pack", [P, 108])
        dtx = RA[:, 9984:10048].rearrange("p (t h) -> p t h", t=TT)
        dmx = RA[:, 10048:10112].rearrange("p (t h) -> p t h", t=TT)
        dna = RA[:, 10112:10176].rearrange("p (t h) -> p t h", t=TT)
        dt_ = sb("dt_", [P, TT, 16])
        dtA = sb("dtA", [P, TT, 16])
        ea = alog
        acum = sb("acum", [P, TT, 16])
        tot = sb("tot", [P, TT, 16])
        dec = sb("dec", [P, TT, 16])
        eac = sb("eac", [P, TT, 16])
        cdec = sb("cdec", [P, TT, 16])
        ss = sb("ss", [P, 32])
        rs = sb("rs", [P, 32])
        wi = sb("wi", [P, TT, 16])
        m8 = sb("m8", [P, 8])
        mx = sb("mx", [P, 4])
        nm = sb("nm", [P, 4])
        sm = sb("sm", [P, 4])
        rc = sb("rc", [P, 4])
        ccol = sb("ccol", [P, KD])
        csil = ccol
        MV = sb("MV", [P, 6, KD])
        bmod = sb("bmod", [P, 6, KD])
        lmod = sb("lmod", [P, 6, KD])
        n1g = sb("n1g", [P, KD])
        n2g = sb("n2g", [P, KD])
        G1 = sb("G1", [P, KD])
        G2 = sb("G2", [P, KD])
        bst = RA[:, 6144:6240].rearrange("p (t c s) -> p t c s", t=TT, c=4)
        mv = sb("mv", [P, TT, 2])
        gmg = RG[:, 2048:2560]
        WS = RG[:, 2560:3072].rearrange("p (g t) -> p g t", g=4)
        WR = RG[:, 3072:3648].rearrange("p (k e) -> p k e", k=KD)
        br = sb("br", [P, 36])
        L = RA[:, 6144:6288].rearrange("p (t e) -> p t e", t=TT)
        r4 = RA[:, 7168:7184].rearrange("p (t g) -> p t g", g=4)
        oh = RA[:, 7184:7200].rearrange("p (t g) -> p t g", g=4)
        gm1 = sb("gm1", [P, TT])
        pg = sb("pg", [P, TT])
        el3 = RA[:, 6288:6416].rearrange("p (t g e) -> p t g e", t=TT, g=4)
        el = RA[:, 6416:6448].rearrange("p (t e) -> p t e", t=TT)
        o1 = RA[:, 6448:6480].rearrange("p (t e) -> p t e", t=TT)
        o2 = RA[:, 6480:6512].rearrange("p (t e) -> p t e", t=TT)
        tmx = sb("tmx", [P, TT])
        e1v = sb("e1v", [P, TT])
        e2v = sb("e2v", [P, TT])
        wa = sb("wa", [P, TT])
        wb = sb("wb", [P, TT])
        E1 = RA[:, 6512:6640].rearrange("p (t e) -> p t e", t=TT)
        E2 = RA[:, 6640:6768].rearrange("p (t e) -> p t e", t=TT)
        EM = RA[:, 6768:6896].rearrange("p (t e) -> p t e", t=TT)
        nbk = sb("nbk", [P, NE])
        bend = sb("bend", [P, NE])
        slot = RA[:, 6896:7024].rearrange("p (t e) -> p t e", t=TT)
        sl = sb("sl", [P, 2, TT])
        sli = sb("sli", [P, 2, TT], I32)
        toki = sb("toki", [P, TT], I32)
        blke = RA[0:1, 1792:1840]
        blki = sb("blki", [1, NBLK], I32)
        nbi = sb("nbi", [1, 1], I32)
        zidx = RM[:, 2048:2048 + NBLK * BLK // P].bitcast(I32)
        IDX = [sb(f"IDX{u}", [BLK, 1], I32) for u in range(2)]

        gates_d = nc.dram_tensor("gates_d", (2, D), F32, kind="Internal").ap()
        xn2_d = nc.dram_tensor("xn2_d", (S, D), F32, kind="Internal").ap()
        slot_d = nc.dram_tensor("slot_d", (NBLK * BLK, 1), I32, kind="Internal").ap()
        ys_d = nc.dram_tensor("ys_d", (NBLK * BLK, D), F32, kind="Internal").ap()

        w_in, w_out, w_in2, w_out2 = a["w_in"][0], a["w_out"][0], a["w_in_2"][0], a["w_out_2"][0]
        chunks = [("xbc", w_in, C_XBC + 512 * i, 512, 16, False) for i in range(4)]
        chunks += [("z", w_in, C_Z + 512 * i, 512, 16, True) for i in range(2)]
        chunks += [("small", w_in, None, 96, 16, True)]
        chunks += [("q", w_in, C_Q + 512 * i, 512, 16, True) for i in range(2)]
        chunks += [("kv", w_in, C_K, 512, 16, True)]
        chunks += [("qi", w_in, C_QI + 512 * i, 512, 16, True) for i in range(2)]
        chunks += [("za", w_in, C_ZA + 512 * i, 512, 16, False) for i in range(2)]
        chunks += [("out", w_out, 512 * i, 512, 16, True) for i in range(4)]
        chunks += [(k, w_in2, c, 512, 16, True) for k, c in (("va", 512), ("ua", 0), ("q2", 1024), ("k2", 1536), ("v2", 2048))]
        chunks += [("out2", w_out2, 512 * i, 512, 8, True) for i in range(4)]
        first = {}
        for n, ch in enumerate(chunks):
            first.setdefault(ch[0], n)

        loads, load_of = [], {}
        landed = [0, 0, 0, 0]
        for c, ch in enumerate(chunks):
            for q in range(ch[4] // 4):
                n = len(loads)
                landed[n % 4] += 32 if ch[0] == "small" else 16
                load_of[c, q] = (n % 4, landed[n % 4])
                loads.append((c, q))

        use, times = {}, [0] * 8

        def plan(key, b):
            use[key] = (b, times[b])
            times[b] += 1

        aux = [0]

        def plan_aux(key):
            plan(key, 4 + aux[0] % 4)
            aux[0] += 1

        def posts(c):
            kind = chunks[c][0]
            i = c - first[kind]
            if kind == "xbc":
                return [("T", c, j) for j in range(4)] if i < 3 else []
            if kind == "small":
                return [("T", c, 0)]
            if kind in ("q", "qi", "q2", "k2"):
                return [("T", c, j) for j in range(4)]
            if kind == "kv":
                return [("T", c, j) for j in range(2)]
            return []

        MODSUM = {3 * (v + 1): v for v in range(6)}
        STAGES = [list(range(0, 7)), list(range(7, 14)), list(range(14, 18)), list(range(18, 23)), list(range(23, 27))]
        SBJ = [(h, j) for h in range(4) for j in range(4)]
        for kt in range(KD):
            plan_aux(("xT", kt))
        plan_aux("pack")
        for n, stage in enumerate(STAGES):
            for c in stage:
                for j in range(4):
                    plan(("P", c, j), j)
                if c in MODSUM:
                    plan_aux(("mod", MODSUM[c]))
                if c > stage[0]:
                    for k in posts(c - 1):
                        plan_aux(k)
            for k in posts(stage[-1]):
                plan_aux(k)
            if n == 0:
                plan("cum", 6)
                for i in range(16):
                    plan(("G", i), i % 2)
                    plan(("AC", i), 2 + i % 2)
                    plan(("Y", i), 4 + i % 2)
                    if i < 12:
                        plan(("ST", i), 6 + i % 2)
                for ct in range(8):
                    plan_aux(("ZT", ct))
            if n == 1:
                for i in range(TT):
                    if i:
                        for hd in range(IH):
                            plan(("IX", i, hd), hd % 4)
                    for g in range(KVH):
                        for r in range(4):
                            plan(("S", i, 4 * g + r), r)
                        for kb in range(i + 1):
                            plan(("PT", i, g, kb), 4 + kb % 3)
                        plan(("PV", i, g), 7)
            if n == 2:
                for kt in range(KD):
                    plan_aux(("hT", kt))
                plan_aux("wsT")
            if n == 3:
                for tt in range(TT):
                    plan_aux(("SPG", tt))
                for h in range(4):
                    for j in range(4):
                        plan(("Z", h, j), 4 * (h % 2) + j)
                    plan(("O", h), 4 * (h % 2))
                for ct in range(8):
                    plan_aux(("yT", ct))
            if n == 4:
                for kt in range(KD):
                    plan_aux(("h2T", kt))
                plan_aux("router")
                plan_aux("rank")

        bank_full = [sem(f"bank_full{i}") for i in range(8)]
        bank_free = [sem(f"bank_free{i}") for i in range(8)]

        def filled(eng, key):
            b, n = use[key]
            eng.wait_ge(bank_full[b], n + 1)
            return ps[b]

        def freed(key):
            b, n = use[key]
            return bank_free[b], n + 1

        phase = {k: sem("phase_" + k) for k in ("pe", "act", "dve", "pool", "sp")}
        phases = {k: 0 for k in phase}

        def barrier(eng, me, who=("pe", "act", "dve")):
            eng.sem_inc(phase[me], 1)
            phases[me] += 1
            for o in who:
                if o != me:
                    eng.wait_ge(phase[o], phases[me])

        small_landed = sem("small_landed")
        x_landed = sem("x_landed")
        slot_free = sem("slot_free")
        w_landed = [sem(f"w_landed{i}") for i in range(4)]
        mod_landed = [sem("mod_landed0"), sem("mod_landed1")]
        mod_used = sem("mod_used")
        mod_ready = sem("mod_ready")
        xT_dve, xT_act = sem("xT_dve"), sem("xT_act")
        SMALL = []
        N_SMALL = 17
        PH_MOE = 10

        block = ctx.enter_context(nc.Block())

        def bcast_row(row):
            return row.partition_broadcast(P)

        @block.sync
        def _(sp):
            ws = a["conv_w"][0].rearrange("t (j p) -> (t j) p", p=P)
            SMALL.append((cst[:, :], a["const"]))
            SMALL.append((ccol[:, :], a["c_2"].rearrange("b (p k) -> (b p) k", k=KD)))
            SMALL.append((packrow[0:64, :], ws))
            SMALL.append((packrow[64:80, :], a["conv_b"].rearrange("l (j p) -> (l j) p", p=P)))
            SMALL.append((packrow[80:88, :], a["ssd_norm_w"].rearrange("l (j p) -> (l j) p", p=P)))
            SMALL.append((packrow[88:96, :], a["out_norm_g_2"].rearrange("l (j p) -> (l j) p", p=P)))
            SMALL.append((packrow[96:97, :], a["q_norm_g_2"]))
            SMALL.append((packrow[97:98, :], a["k_norm_g_2"]))
            SMALL.append((packrow[98:102, :], a["gm_bs_2"][0]))
            SMALL.append((dtb[:, :], bcast_row(a["dt_bias"][0])))
            SMALL.append((alog[:, :], bcast_row(a["a_log"][0])))
            SMALL.append((dsk[:, :], bcast_row(a["d_skip"][0])))
            SMALL.append((bmod[:, :, :], a["b_mod_2"].rearrange("(v p k) -> p v k", v=6, k=KD)))
            SMALL.append((lmod[:, :, :], a["mod_layer_2"][0].rearrange("(v p k) -> p v k", v=6, k=KD)))
            SMALL.append((n1g[:, :], a["norm1_g_2"][0].rearrange("(p k) -> p k", k=KD)))
            SMALL.append((n2g[:, :], a["norm2_g_2"][0].rearrange("(p k) -> p k", k=KD)))
            SMALL.append((br[:, 0:4], bcast_row(a["b_group_2"][0])))
            SMALL.append((br[:, 4:36], bcast_row(a["b_route_2"][0])))
            sp.dma_start(*SMALL[0]).then_inc(sem("const_landed"), 16)
            n = 0
            for c, q in loads:
                kind, w, col, width, kk, _ = chunks[c]
                if n >= 4:
                    sp.wait_ge(slot_free, n - 3)
                if kk == 16 and w.tensor.name != a["w_out"].tensor.name:
                    rows = w.rearrange("(p k) n -> p k n", k=KD)
                else:
                    rows = w.rearrange("(k p) n -> p k n", p=P)
                if kind == "small":
                    sp.dma_start(W[:, n % 4, :, 0:80], rows[:, 4 * q:4 * q + 4, C_KI:C_KI + 80]).then_inc(w_landed[n % 4], 16)
                    sp.dma_start(W[:, n % 4, :, 80:96], rows[:, 4 * q:4 * q + 4, C_DT:C_DT + 16]).then_inc(w_landed[n % 4], 16)
                else:
                    sp.dma_start(W[:, n % 4, :, :], rows[:, 4 * q:4 * q + 4, col:col + 512]).then_inc(w_landed[n % 4], 16)
                n += 1
                if n == 4:
                    for dst, src in SMALL[1:]:
                        sp.dma_start(dst, src).then_inc(small_landed, 16)
            sp.wait_ge(sem("routed"), 1)
            for me in ("pe", "act", "dve"):
                sp.wait_ge(phase[me], PH_MOE)
            blocks = sp.value_load(nbi[0:1, 0:1], min_val=1, max_val=NBLK)
            wgv = a["w_gate_2"][0].rearrange("e (p k) n -> e p k n", k=KD)
            wuv = a["w_up_2"][0].rearrange("e (p k) n -> e p k n", k=KD)
            wdv = a["w_down_2"][0].rearrange("e (m p) n -> e p m n", p=P)
            with sp.Fori(0, NBLK // 2) as i:
                with sp.If(i * 2 < blocks):
                    for u in range(2):
                        e = sp.value_load(blki[0:1, bass.ds(i * 2 + u, 1)], min_val=0, max_val=NE - 1)
                        sp.wait_ge(sem(f"up_done{u}"), i)
                        sp.dma_start(WGt[u], wgv[e]).then_inc(sem(f"wg_landed{u}"), 16)
                        sp.dma_start(WUt[u], wuv[e]).then_inc(sem(f"wu_landed{u}"), 16)
                        sp.wait_ge(sem(f"down_done{u}"), i)
                        sp.dma_start(WDt[u], wdv[e]).then_inc(sem(f"wd_landed{u}"), 16)

        @block.gpsimd
        def _(pool):
            st = Steps(pool, sem("pool_done"))
            st.do(nc.gpsimd.memset(zidx[:, :], 0))
            st.settle()
            pool.dma_start(slot_d.rearrange("(p n) o -> p (n o)", p=P), zidx[:, :]).then_inc(sem("idx_cleared"), 16)
            st.do(nc.gpsimd.memset(RM[:, 0:D], 0.0))
            st.settle()
            spare = ys_d[16 * BLK:, :].rearrange("(n p) d -> p n d", p=P)
            pool.dma_start(spare, RM[:, 0:D].unsqueeze(1).to_broadcast([P, (NBLK - 16) * BLK // P, D])).then_inc(sem("ys_cleared"), 16)
            wm = a["w_mod_2"].rearrange("(p k) n -> p k n", k=KD)
            for s in range(6 * KD):
                v, kt = divmod(s, KD)
                if s >= 2:
                    pool.wait_ge(mod_used, s - 1)
                pool.dma_start(mring[:, s % 2, :], wm[:, kt, v * D:(v + 1) * D]).then_inc(mod_landed[s % 2], 16)
            pool.wait_ge(sem("routed"), 1)
            pool.wait_ge(sem("idx_cleared"), 16)
            for k in range(2):
                for tt in range(TT):
                    pool.indirect_dma_start(out=slot_d, out_offset=bass.IndirectOffsetOnAxis(ap=sli[:, k, tt:tt + 1], axis=0),
                                            in_=toki[:, tt:tt + 1], in_offset=None).then_inc(sem("idx_stored"), 16)
            pool.wait_ge(sem("idx_stored"), 128)
            pool.wait_ge(sem("xn_stored"), 16)
            for me in ("pe", "act", "dve"):
                pool.wait_ge(phase[me], PH_MOE)
            blocks = pool.value_load(nbi[0:1, 0:1], min_val=1, max_val=NBLK)
            slot_rows = slot_d.rearrange("(b s) o -> b s o", s=BLK)
            with pool.Fori(0, NBLK // 2) as i:
                with pool.If(i * 2 < blocks):
                    for u in range(2):
                        pool.wait_ge(sem(f"xg_landed{u}"), i * 16)
                        pool.dma_start(IDX[u][:, :], slot_rows[i * 2 + u]).then_inc(sem(f"id_landed{u}"), 16)
                        pool.wait_ge(sem(f"id_landed{u}"), i * 16 + 16)
                        pool.wait_ge(sem(f"t_done{u}"), i)
                        pool.sem_inc(sem("pool_passed"), 1)
                        pool.indirect_dma_start(out=xg[u], out_offset=None, in_=xn2_d,
                                                in_offset=bass.IndirectOffsetOnAxis(ap=IDX[u][:, 0:1], axis=0)).then_inc(sem(f"xg_landed{u}"), 16)
            for me in ("act", "dve", "pe"):
                pool.wait_ge(phase[me], PH_MOE + 1)
            for tt in range(TT):
                if tt >= 2:
                    pool.wait_ge(sem("picked_used"), tt - 1)
                for k in range(2):
                    pool.indirect_dma_start(out=picked[tt % 2][k], out_offset=None, in_=ys_d,
                                            in_offset=bass.IndirectOffsetOnAxis(ap=sli[:, k, tt:tt + 1], axis=0)).then_inc(sem(f"picked_landed{tt % 2}"), 16)

        @block.tensor
        def _(pe):
            def claim(key):
                b, n = use[key]
                if n:
                    pe.wait_ge(bank_free[b], n)
                return ps[b]

            def full(ins, key):
                ins.then_inc(bank_full[use[key][0]], 1)
                last[0] = (bank_full[use[key][0]], use[key][1] + 1)

            last = [None]

            def bar():
                pe.wait_ge(*last[0])
                barrier(pe, "pe")

            def transposes(key, srcs):
                bk = claim(key)
                for n, src in enumerate(srcs):
                    ins = nc.tensor.transpose(bk[0:src.shape[1], n * P:n * P + src.shape[0]], src, ident[0:src.shape[0], 0:src.shape[0]])
                full(ins, key)

            def project(c):
                kind, w, col, width, kk, token_major = chunks[c]
                act = {"out": M, "out2": yT}.get(kind, X)
                banks = []
                for kt in range(kk):
                    s, count = load_of[c, kt // 4]
                    if kt % 4 == 0:
                        pe.wait_ge(w_landed[s], count)
                    for j in range(4):
                        key = ("P", c, j)
                        if kt == 0:
                            banks.append(claim(key))
                        if token_major:
                            ins = nc.tensor.matmul(banks[j][:, 0:width], act[:, kt, j * P:(j + 1) * P], W[:, s, kt % 4, 0:width],
                                                   start=kt == 0, stop=kt == kk - 1)
                        else:
                            ins = nc.tensor.matmul(banks[j][:, :], W[:, s, kt % 4, j * P:(j + 1) * P], act[:, kt, :],
                                                   start=kt == 0, stop=kt == kk - 1)
                        if kt == kk - 1:
                            full(ins, key)
                            if j == 3:
                                pe.wait_ge(*last[0])
                                pe.sem_inc(slot_free, 1)
                        elif kt % 4 == 3 and j == 3:
                            ins.then_inc(slot_free, 1)

            def mod_sum(v):
                bk = claim(("mod", v))
                pe.wait_ge(mod_ready, v + 1)
                for kt in range(KD):
                    ins = nc.tensor.matmul(bk[:, kt:kt + 1], macc[:, kt:D:KD], C["ones"][:, 0:1], start=True, stop=True)
                full(ins, ("mod", v))

            def post(c):
                kind = chunks[c][0]
                i = c - first[kind]
                for key in posts(c):
                    j = key[2]
                    if kind == "xbc":
                        pe.wait_ge(sem("silu_done"), 4 * i + j + 1)
                        src = SL[:, j, :] if i < 2 else bfm[:, j, :]
                        transposes(key, [src[:, tt * P:(tt + 1) * P] for tt in range(TT)])
                    elif kind == "small":
                        pe.wait_ge(sem("ki_ready"), 1)
                        transposes(key, [TK[:, tt, :] for tt in range(TT)])
                    elif kind in ("q2", "k2"):
                        pe.wait_ge(sem("norm_ready"), 2 if kind == "k2" else 1)
                        transposes(key, [T2[:, tt, j * P:(j + 1) * P] for tt in range(TT)])
                    else:
                        pe.wait_ge(sem("rope_ready"), c - first["q"] + 1)
                        transposes(key, [T[:, tt, j * P:(j + 1) * P] for tt in range(TT)])

            def stage(n):
                for c in STAGES[n]:
                    project(c)
                    if c in MODSUM:
                        mod_sum(MODSUM[c])
                    if c > STAGES[n][0]:
                        post(c - 1)
                post(STAGES[n][-1])

            pe.wait_ge(sem("const_landed"), 16)
            for tt in range(TT):
                pe.wait_ge(x_landed, 16 * TT)
            for kt in range(KD):
                transposes(("xT", kt), [Hx[:, tt, kt, :] for tt in range(TT)])
            pe.wait_ge(small_landed, 16 * N_SMALL)
            transposes("pack", [packrow[0:102, :]])
            pe.wait_ge(xT_dve, 8)
            pe.wait_ge(xT_act, 8)
            stage(0)
            bar()

            bk = claim("cum")
            pe.wait_ge(sem("dtA_ready"), 1)
            flat = dtA[:, :, :].rearrange("p t h -> p (t h)")
            nc.tensor.matmul(bk[:, 0:64], C["upto"], flat, start=True, stop=True)
            full(nc.tensor.matmul(bk[:, 64:128], C["ones"], flat, start=True, stop=True), "cum")

            def ssd_front(i):
                c, g = divmod(i, SG)
                bk = claim(("G", i))
                full(nc.tensor.matmul(bk[:, 0:P], bfm[:, g, c * P:(c + 1) * P], cfm[:, g, c * P:(c + 1) * P], start=True, stop=True), ("G", i))
                bk = claim(("AC", i))
                for r in range(SR):
                    ins = nc.tensor.matmul(bk[:, r * P:(r + 1) * P], dtA[:, c, 4 * g + r:4 * g + r + 1].to_broadcast([P, P]), C["upto"],
                                           start=True, stop=True)
                full(ins, ("AC", i))

            def ssd_back(i):
                c, g = divmod(i, SG)
                bk = claim(("Y", i))
                pe.wait_ge(sem("decay_ready"), i + 1)
                for r in range(SR):
                    h = 4 * g + r
                    ins = nc.tensor.matmul(bk[:, r * 64:(r + 1) * 64], Mt[:, i % 2, r, :], xdt[:, c % 2, h * 64:(h + 1) * 64], start=True, stop=True)
                if c:
                    pe.wait_ge(sem("state_ready"), i - 3)
                    ins = nc.tensor.matmul(bk[:, 256:512], cfm[:, g, c * P:(c + 1) * P], Hst[:, g * 256:(g + 1) * 256], start=True, stop=True)
                full(ins, ("Y", i))
                if i < 12:
                    bk = claim(("ST", i))
                    full(nc.tensor.matmul(bk[:, 0:256], btm[:, c, g * P:(g + 1) * P], xdd[:, c % 2, g * 256:(g + 1) * 256], start=True, stop=True), ("ST", i))

            ssd_front(0)
            for i in range(16):
                if i < 15:
                    ssd_front(i + 1)
                ssd_back(i)
            for ct in range(8):
                pe.wait_ge(sem("gated_ready"), 16)
                transposes(("ZT", ct), [Z[:, tt, ct * P:(ct + 1) * P] for tt in range(TT)])
            bar()
            stage(1)
            bar()

            for i in range(TT):
                nk = (i + 1) * P
                if i:
                    for hd in range(IH):
                        key = ("IX", i, hd)
                        bk = claim(key)
                        lo = 64 * (hd % 2)
                        full(nc.tensor.matmul(bk[:, 0:nk], qiT[lo:lo + 64, hd // 2, i * P:(i + 1) * P], kiT[lo:lo + 64, 0:nk],
                                              start=True, stop=True), key)
                for g in range(KVH):
                    for r in range(4):
                        key = ("S", i, 4 * g + r)
                        bk = claim(key)
                        full(nc.tensor.matmul(bk[:, 0:nk], qT[:, 4 * g + r, i * P:(i + 1) * P], kT[:, g, 0:nk], start=True, stop=True), key)
                    pe.wait_ge(sem("probs_ready"), 2 * i + g + 1)
                    for kb in range(i + 1):
                        transposes(("PT", i, g, kb), [Pb[:, r, kb * P:(kb + 1) * P] for r in range(4)])
                    bk = claim(("PV", i, g))
                    for kb in range(i + 1):
                        pe.wait_ge(sem("pt_ready"), sum(2 * (x + 1) for x in range(i)) + g * (i + 1) + kb + 1)
                        ins = nc.tensor.matmul(bk[:, :], V[:, kb, g * P:(g + 1) * P], PT[:, kb, :], start=kb == 0, stop=kb == i)
                    full(ins, ("PV", i, g))
            bar()
            stage(2)
            bar()
            pe.wait_ge(sem("xn_ready"), 4)
            for kt in range(KD):
                transposes(("hT", kt), [XNx[:, tt, kt, :] for tt in range(TT)])
            pe.wait_ge(sem("late_landed"), 64)
            transposes("wsT", [WS[:, g, :] for g in range(4)])
            bar()
            stage(3)
            bar()

            for tt in range(TT):
                bk = claim(("SPG", tt))
                for g in range(4):
                    ins = nc.tensor.matmul(bk[:, g * P:(g + 1) * P], WS[:, g, :], VA[:, tt, g * P:(g + 1) * P], start=True, stop=True)
                full(ins, ("SPG", tt))
            for h in range(4):
                for j in range(4):
                    bk = claim(("Z", h, j))
                    n = S - P * j
                    full(nc.tensor.matmul(bk[:, 0:n], kT2[:, h, j * P:(j + 1) * P], qT2[:, h, j * P:S], start=True, stop=True), ("Z", h, j))
                for j in range(4):
                    bk = ps[use["Z", h, j][0]]
                    n = S - P * j
                    pe.wait_ge(sem("fail_ready"), 4 * h + 4)
                    for jj in range(j, 4):
                        nc.tensor.matmul(bk[:, (jj - j) * P:n], C["neg_from"] if jj == j else C["neg_ones"], SPl[jj],
                                         start=False, stop=False, skip_group_check=True)
                    ins = nc.tensor.matmul(bk[:, 0:P], ident, C["not_before"], start=False, stop=True, skip_group_check=True)
                    ins.then_inc(sem("log_a_ready"), 1)
                pe.wait_ge(sem("a_ready"), 4 * h + 4)
                bk = claim(("O", h))
                for i in range(TT):
                    for j in range(i + 1):
                        ins = nc.tensor.matmul(bk[:, i * P:(i + 1) * P], AT[j][:, (i - j) * P:(i - j + 1) * P], V2[:, j, h * P:(h + 1) * P],
                                               start=j == 0, stop=j == i)
                full(ins, ("O", h))
            pe.wait_ge(sem("y_ready"), 1)
            for ct in range(8):
                transposes(("yT", ct), [Y[:, tt, ct * P:(ct + 1) * P] for tt in range(TT)])
            bar()
            stage(4)
            bar()
            pe.wait_ge(sem("xn_ready"), 8)
            for kt in range(KD):
                transposes(("h2T", kt), [XNx[:, tt, kt, :] for tt in range(TT)])
            pe.wait_ge(sem("h2T_dve"), 8)
            pe.wait_ge(sem("h2T_act"), 8)
            bk = claim("router")
            for tt in range(TT):
                for kt in range(KD):
                    ins = nc.tensor.matmul(bk[:, tt * 36:(tt + 1) * 36], X[:, kt, tt * P:(tt + 1) * P], WR[:, kt, :], start=kt == 0, stop=kt == KD - 1)
            full(ins, "router")
            pe.wait_ge(sem("choice_ready"), 1)
            bk = claim("rank")
            for tt in range(TT):
                for s in range(tt + 1):
                    nc.tensor.matmul(bk[:, tt * NE:(tt + 1) * NE], C["before"] if s == tt else C["ones"], EM[:, s, :], start=s == 0, stop=s == tt)
            for s in range(TT):
                ins = nc.tensor.matmul(bk[:, P:P + NE], C["ones"], EM[:, s, :], start=s == 0, stop=s == TT - 1)
            full(ins, "rank")
            bar()

            pe.wait_ge(sem("routed"), 1)
            blocks = pe.value_load(nbi[0:1, 0:1], min_val=1, max_val=NBLK)
            with pe.Fori(0, NBLK // 2) as i:
                with pe.If(i * 2 < blocks):
                    for u in range(2):
                        pe.wait_ge(sem(f"xg_landed{u}"), i * 16 + 16)
                        pe.wait_ge(sem("t_taken"), i * 2 + u)
                        pe.sem_inc(sem("pe_passed"), 1)
                        for kt in range(KD):
                            ins = nc.tensor.transpose(ps[kt // 8][:, (kt % 8) * BLK:(kt % 8 + 1) * BLK], xgx[u][:, kt, :], ident[0:BLK, 0:BLK])
                        ins.then_inc(sem(f"t_done{u}"), 1)
                        pe.wait_ge(sem(f"xt_ready"), i * 2 + u + 1)
                        pe.wait_ge(sem("h_ready"), i * 2 + u)
                        for w, bk, land in ((WGt[u], ps[2], f"wg_landed{u}"), (WUt[u], ps[3], f"wu_landed{u}")):
                            pe.wait_ge(sem(land), i * 16 + 16)
                            for m in range(2):
                                for kt in range(KD):
                                    ins = nc.tensor.matmul(bk[:, m * BLK:(m + 1) * BLK], w[:, kt, m * P:(m + 1) * P], xgT[u][:, kt, :],
                                                           start=kt == 0, stop=kt == KD - 1)
                        ins.then_inc(sem(f"up_done{u}"), 1)
                        pe.wait_ge(sem("h_ready"), i * 2 + u + 1)
                        pe.wait_ge(sem(f"wd_landed{u}"), i * 16 + 16)
                        pe.wait_ge(sem("y_taken_dve"), i * 2 + u)
                        pe.wait_ge(sem("y_taken_act"), i * 2 + u)
                        for n in range(4):
                            for m in range(2):
                                ins = nc.tensor.matmul(ps[4 + n][0:BLK, :], hb[u][:, m, :], WDt[u][:, m, n * 512:(n + 1) * 512], start=m == 0, stop=m == 1)
                        ins.then_inc(sem(f"down_done{u}"), 1)
            pe.sem_inc(phase["pe"], 1)

        @block.scalar
        def _(act):
            st = Steps(act, sem("act_done"))

            def fn(dst, src, func, s=None, v=None, **kw):
                st.do(nc.scalar.activation(dst, src, func, **kw), s, v)

            def bar():
                st.settle()
                barrier(act, "act")

            for tt in range(TT):
                act.dma_start(H[:, tt, :], a["x"][0, tt * P:(tt + 1) * P, :]).then_inc(x_landed, 16)
            act.wait_ge(small_landed, 16 * N_SMALL)
            fn(csil[:, :], ccol[:, :], ACT.Silu, sem("csil_ready"))
            for kt in range(1, KD, 2):
                bk = filled(act, ("xT", kt))
                fn(X[:, kt, :], bk[:, :], ACT.Copy, *freed(("xT", kt)))
            st.settle()
            act.sem_inc(xT_act, 8)

            def take_post(c):
                kind = chunks[c][0]
                i = c - first[kind]
                for key in posts(c):
                    j = key[2]
                    bk = filled(act, key)
                    if kind == "xbc":
                        src = bk[:, :].rearrange("p (t e) -> p t e", t=TT)
                        dst = xs[:, :, (4 * i + j) * P:(4 * i + j + 1) * P] if i < 2 else btm[:, :, j * P:(j + 1) * P]
                        fn(dst, src, ACT.Copy, *freed(key))
                    elif kind == "small":
                        fn(kiT, bk[:, :], ACT.Copy, *freed(key))
                    elif kind == "q":
                        fn(qT[:, 4 * i + j, :], bk[:, :], ACT.Copy, *freed(key))
                    elif kind == "kv":
                        fn(kT[:, j, :], bk[:, :], ACT.Copy, *freed(key))
                    elif kind == "qi":
                        fn(qiT[:, 4 * i + j, :], bk[:, :], ACT.Copy, *freed(key))
                    elif kind == "q2":
                        fn(qT2[:, j, :], bk[:, :], ACT.Copy, *freed(key), scale=pack[:, 102:103])
                    elif kind == "k2":
                        fn(kT2[:, j, :], bk[:, :], ACT.Copy, *freed(key), scale=pack[:, 97:98])

            def work(c):
                kind = chunks[c][0]
                i = c - first[kind]
                for j in range(4):
                    key = ("P", c, j)
                    if kind == "xbc":
                        act.wait_ge(sem("conv_done"), 4 * i + j + 1)
                        dst = SL[:, j, :] if i < 2 else (bfm if i == 2 else cfm)[:, j, :]
                        fn(dst, CV[:, j % 2, :], ACT.Silu, sem("silu_done"))
                    elif kind == "z":
                        if i == 0 and j == 0:
                            act.wait_ge(sem("ys_cleared"), 16)
                            act.wait_ge(sem("idx_cleared"), 16)
                        fn(Z[:, j, i * 512:(i + 1) * 512], filled(act, key)[:, :], ACT.Silu, *freed(key))
                    elif kind == "small":
                        fn(SM[:, j, :], filled(act, key)[:, 0:96], ACT.Copy, *freed(key))
                    elif kind in ("q", "kv", "qi"):
                        bk = filled(act, key)
                        if kind == "kv":
                            fn(V[:, j, :], bk[:, 256:512], ACT.Copy)
                        fn(T[:, j, :], bk[:, :], ACT.Copy, *freed(key))
                    elif kind == "za":
                        fn(M[:, 4 * i + j, :], filled(act, key)[:, :], ACT.Silu, *freed(key))
                    elif kind in ("va", "ua"):
                        fn((VA if kind == "va" else UA)[:, j, :], filled(act, key)[:, :], ACT.Gelu, *freed(key))
                    elif kind in ("q2", "k2"):
                        bk = filled(act, key)
                        fn(T2[:, j, :], bk[:, :], ACT.Copy)
                        fn(SQ[:, j, :], bk[:, :], ACT.Square, *freed(key))
                    elif kind == "v2":
                        fn(V2[:, j, :], filled(act, key)[:, :], ACT.Copy, *freed(key))
                if kind in ("small", "q", "kv", "qi", "va", "q2", "k2"):
                    st.settle()
                    act.sem_inc(sem("copied"), 1)
                if kind in ("va", "q2", "k2"):
                    act.wait_ge(sem("mean_ready"), ("va", "q2", "k2").index(kind) + 1)
                    fn(rs[:, 0:16], rs[:, 0:16], ACT.Sqrt, sem("root_ready"))

            def stage(n):
                for c in STAGES[n]:
                    if c > STAGES[n][0]:
                        take_post(c - 1)
                    work(c)
                take_post(STAGES[n][-1])

            stage(0)
            bar()
            act.wait_ge(sem("dt_in"), 1)
            fn(dna[:, :, :], dna[:, :, :], ACT.Exp)
            fn(ea[:, :], alog[:, :], ACT.Exp)
            st.settle()
            fn(dna[:, :, :], dna[:, :, :], ACT.Ln, sem("dt_log"), bias=1.0)
            act.wait_ge(sem("cum_ready"), 1)
            fn(eac[:, :, :], acum[:, :, :], ACT.Exp)
            fn(cdec[:, :, :], tot[:, :, :], ACT.Exp)
            fn(dec[:, :, :], dec[:, :, :], ACT.Exp, sem("cum_exp"))
            for i in range(16):
                act.wait_ge(sem("diff_ready"), i + 1)
                fn(Dm[:, i % 2, :, :], Dm[:, i % 2, :, :], ACT.Exp, sem("diff_exp"))
            act.wait_ge(sem("ms_ready"), 1)
            fn(rs[:, 0:16], rs[:, 0:16], ACT.Sqrt, sem("ms_root"))
            for ct in range(8):
                fn(M[:, 8 + ct, :], filled(act, ("ZT", ct))[:, :], ACT.Copy, *freed(("ZT", ct)), scale=pack[:, 80 + ct:81 + ct])
            bar()
            stage(1)
            bar()
            n_relu, n_exp, n_pt = 0, 0, 0
            for i in range(TT):
                nk = (i + 1) * P
                if i:
                    for hd in range(IH):
                        bk = filled(act, ("IX", i, hd))
                        if n_relu >= 2:
                            act.wait_ge(sem("relu_used"), n_relu - 1)
                        fn(R[:, hd % 2, 0:nk], bk[:, 0:nk], ACT.Relu, *freed(("IX", i, hd)))
                        n_relu += 1
                for g in range(KVH):
                    for r in range(4):
                        n_exp += 1
                        act.wait_ge(sem("max_ready"), n_exp)
                        fn(Pb[:, r, 0:nk], Pb[:, r, 0:nk], ACT.Exp, sem("exp_done"), bias=nm[:, r:r + 1], accum_out=sm[:, r:r + 1])
                    for kb in range(i + 1):
                        bk = filled(act, ("PT", i, g, kb))
                        if kb == 0 and (i or g):
                            filled(act, ("PV", i, 0) if g else ("PV", i - 1, 1))
                        fn(PT[:, kb, :], bk[:, :], ACT.Copy, *freed(("PT", i, g, kb)))
                        st.settle()
                        act.sem_inc(sem("pt_ready"), 1)
            bar()
            for tt in range(TT):
                act.dma_start(H[:, tt, :], a["x"][0, tt * P:(tt + 1) * P, :]).then_inc(x_landed, 16)
            act.dma_start(lng, bcast_row(a["ln_g"][0])).then_inc(sem("ln_landed"), 16)
            act.dma_start(lnb, bcast_row(a["ln_b"][0])).then_inc(sem("ln_landed"), 16)
            bar()
            act.dma_start(gmg, bcast_row(a["gm_norm_g_2"][0])).then_inc(sem("late_landed"), 16)
            act.dma_start(WS, a["gm_ws_2"][0].rearrange("g t q -> t g q")).then_inc(sem("late_landed"), 16)
            act.dma_start(WR[:, :, 0:4], a["w_group_2"][0].rearrange("(p k) n -> p k n", k=KD)).then_inc(sem("late_landed"), 16)
            act.dma_start(WR[:, :, 4:36], a["w_route_2"][0].rearrange("(p k) n -> p k n", k=KD)).then_inc(sem("late_landed"), 16)
            act.wait_ge(sem("var_ready"), 1)
            fn(rs[:, 0:4], rs[:, 0:4], ACT.Sqrt, sem("var_root"))

            def norm_hidden(n):
                for tt in range(TT):
                    act.wait_ge(sem("h_rows"), 4 * n + tt + 1)
                    fn(junk, H[:, tt, :], ACT.Square, accum_out=ss[:, tt:tt + 1])
                    st.settle()
                    act.sem_inc(sem("sq_done"), 1)
                act.wait_ge(sem("msq_ready"), n + 1)
                fn(rs[:, 0:4], rs[:, 0:4], ACT.Sqrt, sem("msq_root"))

            norm_hidden(0)
            for kt in range(1, KD, 2):
                key = ("hT", kt)
                fn(X[:, kt, :], filled(act, key)[:, :], ACT.Identity, *freed(key), scale=G1[:, kt:kt + 1], bias=MV[:, 0, kt:kt + 1])
            bar()
            stage(3)
            bar()
            for h in range(4):
                for j in range(4):
                    n = S - P * j
                    k = 4 * h + j
                    act.wait_ge(sem("abs_ready"), k + 1)
                    fn(EA[:, k % 2, 0:n], EA[:, k % 2, 0:n], ACT.Exp)
                    st.settle()
                    fn(EA[:, k % 2, 0:n], EA[:, k % 2, 0:n], ACT.Ln, sem("log_ready"), bias=1.0)
                for j in range(4):
                    k = 4 * h + j
                    act.wait_ge(sem("log_a_ready"), k + 1)
                    if j == 0 and h:
                        filled(act, ("O", h - 1))
                    fn(AT[j], ps[use["Z", h, j][0]][:, 0:S - P * j], ACT.Exp, *freed(("Z", h, j)))
                st.settle()
                act.sem_inc(sem("a_ready"), 4)
            act.wait_ge(sem("mean_ready"), 4)
            fn(rs[:, 0:32], rs[:, 0:32], ACT.Sqrt, sem("root_ready"))
            for ct in range(8):
                key = ("yT", ct)
                fn(yT[:, ct, :], filled(act, key)[:, :], ACT.Copy, *freed(key), scale=pack[:, 88 + ct:89 + ct])
            bar()
            act.wait_ge(sem("mod_out"), 6)
            for n, v in enumerate((2, 5)):
                act.dma_start(gates_d[n].rearrange("(p k) -> p k", k=KD), MV[:, v, :]).then_inc(sem("gate_stored"), 16)
            act.wait_ge(sem("gate_stored"), 32)
            act.dma_start(gate, bcast_row(gates_d[0])).then_inc(sem("gate_landed"), 16)
            bar()
            norm_hidden(1)
            for kt in range(1, KD, 2):
                key = ("h2T", kt)
                fn(X[:, kt, :], filled(act, key)[:, :], ACT.Identity, *freed(key), scale=G2[:, kt:kt + 1], bias=MV[:, 3, kt:kt + 1])
            st.settle()
            act.sem_inc(sem("h2T_act"), 8)
            act.dma_start(xn2_d.rearrange("(t p) d -> p t d", p=P), XN).then_inc(sem("xn_stored"), 16)
            act.wait_ge(sem("group_in"), 1)
            fn(r4[:, :, :], r4[:, :, :], ACT.Exp, sem("group_exp"))
            act.wait_ge(sem("pair_in"), 1)
            fn(e2v[:, :], e2v[:, :], ACT.Exp, sem("pair_exp"))
            act.wait_ge(sem("xn_stored"), 16)
            bar()
            act.wait_ge(sem("routed"), 1)
            blocks = act.value_load(nbi[0:1, 0:1], min_val=1, max_val=NBLK)
            ysb = ys_d.rearrange("(b s) d -> b s d", s=BLK)
            with act.Fori(0, NBLK // 2) as i:
                with act.If(i * 2 < blocks):
                    for u in range(2):
                        act.wait_ge(sem(f"up_done{u}"), i + 1)
                        nc.scalar.activation(SGt[u], ps[2][:, 0:P], ACT.Silu).then_inc(sem("silu_gate"), 1)
                        act.wait_ge(sem(f"down_done{u}"), i + 1)
                        act.wait_ge(sem(f"y_stored{u}"), i * 16)
                        nc.scalar.activation(yb[u][:, 1024:1536], ps[6][0:BLK, :], ACT.Copy)
                        nc.scalar.activation(yb[u][:, 1536:2048], ps[7][0:BLK, :], ACT.Copy).then_inc(sem("y_taken_act"), 1)
                        act.wait_ge(sem("y_taken_act"), i * 2 + u + 1)
                        act.wait_ge(sem("y_taken_dve"), i * 2 + u + 1)
                        act.dma_start(ysb[i * 2 + u], yb[u]).then_inc(sem(f"y_stored{u}"), 16)
            pairs = (blocks + 1) // 2
            act.wait_ge(sem("y_stored0"), pairs * 16)
            act.wait_ge(sem("y_stored1"), pairs * 16)
            act.sem_inc(phase["act"], 1)
            for me in ("dve", "pe"):
                act.wait_ge(phase[me], PH_MOE + 1)
            act.dma_start(gate, bcast_row(gates_d[1])).then_inc(sem("gate_landed"), 16)
            for tt in range(TT):
                act.wait_ge(sem("out_ready"), tt + 1)
                act.dma_start(out[0, tt * P:(tt + 1) * P, :], H[:, tt, :]).then_inc(sem("out_stored"), 16)
            act.wait_ge(sem("out_stored"), 16 * TT)

        @block.vector
        def _(dve):
            v = nc.vector
            st = Steps(dve, sem("dve_done"))

            def bar():
                st.settle()
                barrier(dve, "dve")

            def tt_(dst, x, y, op, s=None, n=None):
                st.do(v.tensor_tensor(dst, x, y, op), s, n)

            def ts(dst, x, s1, s2, op0, op1=None, s=None, n=None):
                if op1 is None:
                    st.do(v.tensor_scalar(dst, x, s1, None, op0), s, n)
                else:
                    st.do(v.tensor_scalar(dst, x, s1, s2, op0, op1), s, n)

            def stt(dst, x, sc, y, op0, op1, s=None, n=None):
                st.do(v.scalar_tensor_tensor(out=dst, in0=x, scalar=sc, in1=y, op0=op0, op1=op1), s, n)

            def per(x, shape):
                return x.unsqueeze(len(x.shape)).to_broadcast(shape)

            mod_step = [0]

            def mod_steps(n):
                for _ in range(n):
                    s = mod_step[0]
                    vec, kt = divmod(s, KD)
                    dve.wait_ge(mod_landed[s % 2], 16 * (s // 2 + 1))
                    if kt == 0:
                        if s:
                            filled(dve, ("mod", vec - 1))
                        ts(macc, mring[:, s % 2, :], csil[:, kt:kt + 1], None, ALU.mult, s=mod_used)
                    else:
                        st.settle()
                        stt(macc, mring[:, s % 2, :], csil[:, kt:kt + 1], macc, ALU.mult, ALU.add, s=mod_used)
                    mod_step[0] += 1
                    if kt == KD - 1:
                        st.settle()
                        dve.sem_inc(mod_ready, 1)

            def mod_take(vec):
                key = ("mod", vec)
                bk = filled(dve, key)
                tt_(MV[:, vec, :], bk[:, 0:KD], bmod[:, vec, :], ALU.add, *freed(key))
                st.settle()
                tt_(MV[:, vec, :], MV[:, vec, :], lmod[:, vec, :], ALU.add, sem("mod_out"))
                st.settle()

            def mod_hook(c):
                if c < 18:
                    mod_steps((6, 5, 5)[c % 3])

            dve.wait_ge(sem("const_landed"), 16)
            dve.wait_ge(small_landed, 16 * N_SMALL)
            for kt in range(0, KD, 2):
                st.do(v.tensor_copy(X[:, kt, :], filled(dve, ("xT", kt))[:, :]), *freed(("xT", kt)))
            st.settle()
            dve.sem_inc(xT_dve, 8)
            st.do(v.tensor_copy(pack[:, 0:102], filled(dve, "pack")[:, 0:102]), *freed("pack"))
            st.settle()
            ts(pack[:, 102:103], pack[:, 96:97], float(DH) ** -0.5, None, ALU.mult)
            dve.wait_ge(sem("csil_ready"), 1)

            def rotate(view, cos, sin, heads, half):
                for tt in range(TT):
                    x = view[:, tt]
                    n = heads * 2 * half
                    A = RT[:, 0, 0:n].rearrange("p (h d) -> p h d", h=heads)
                    B = RT[:, 1, 0:n].rearrange("p (h d) -> p h d", h=heads)
                    co = C[cos][:, tt * 2 * half:(tt + 1) * 2 * half].unsqueeze(1).to_broadcast([P, heads, 2 * half])
                    si = C[sin][:, tt * 2 * half:(tt + 1) * 2 * half].unsqueeze(1).to_broadcast([P, heads, 2 * half])
                    tt_(A, x, co, ALU.mult)
                    tt_(B, x, si, ALU.mult)
                    st.settle()
                    tt_(x[:, :, 0:half], A[:, :, 0:half], B[:, :, half:2 * half], ALU.add)
                    tt_(x[:, :, half:2 * half], A[:, :, half:2 * half], B[:, :, 0:half], ALU.add)
                    st.settle()

            def inv_mean(dst, src, n, eps, s):
                ts(dst, src, 1.0 / n, eps, ALU.mult, ALU.add)
                st.settle()
                st.do(v.reciprocal(dst, dst), s)

            def work(c):
                kind = chunks[c][0]
                i = c - first[kind]
                if kind == "xbc":
                    for j in range(4):
                        key = ("P", c, j)
                        bk = filled(dve, key)
                        e = 4 * i + j
                        if e >= 2:
                            dve.wait_ge(sem("silu_done"), e - 1)
                        y = CV[:, j % 2, :]
                        ts(y, bk[:, :], pack[:, 48 + e:49 + e], pack[:, 64 + e:65 + e], ALU.mult, ALU.add)
                        for k in (1, 2, 3):
                            st.settle()
                            stt(y[:, k:S], bk[:, 0:S - k], pack[:, 16 * (3 - k) + e:16 * (3 - k) + e + 1], y[:, k:S], ALU.mult, ALU.add,
                                *(freed(key) if k == 3 else (None, None)))
                        st.settle()
                        dve.sem_inc(sem("conv_done"), 1)
                elif kind == "small":
                    dve.wait_ge(sem("copied"), 1)
                    for half in range(2):
                        st.do(v.tensor_copy(TK[:, :, 64 * half:64 * half + 64], SM[:, :, 0:64]))
                    ts(wi[:, :, :], SM[:, :, 64:80], 1.0 / 32, None, ALU.mult)
                    st.settle()
                    rotate(TK[:, :, :].rearrange("p t (h d) -> p t h d", h=2)[:, :, :, 0:16], "cos_i", "sin_i", 2, 8)
                    dve.sem_inc(sem("ki_ready"), 1)
                elif kind in ("q", "kv", "qi"):
                    dve.wait_ge(sem("copied"), c - first["q"] + 2)
                    if kind == "q":
                        rotate(T[:, :, :].rearrange("p t (h d) -> p t h d", h=4)[:, :, :, 0:32], "cos_a", "sin_a", 4, 16)
                    elif kind == "kv":
                        rotate(T[:, :, 0:256].rearrange("p t (h d) -> p t h d", h=2)[:, :, :, 0:32], "cos_a", "sin_a", 2, 16)
                    else:
                        rotate(T[:, :, :].rearrange("p t (h d) -> p t h d", h=8)[:, :, :, 0:16], "cos_i", "sin_i", 8, 8)
                    dve.sem_inc(sem("rope_ready"), 1)
                elif kind == "out":
                    if i == 0:
                        dve.wait_ge(x_landed, 32 * TT)
                    for tt in range(TT):
                        key = ("P", c, tt)
                        part = H[:, tt, i * 512:(i + 1) * 512]
                        stt(part, part, ALPHA, filled(dve, key)[:, :], ALU.mult, ALU.add, *freed(key))
                        st.settle()
                        st.do(v.bn_stats(bst[:, tt, i, :], part))
                elif kind in ("va", "q2", "k2"):
                    n = ("va", "q2", "k2").index(kind)
                    dve.wait_ge(sem("copied"), 7 + n)
                    if kind == "va":
                        tt_(SQ, VA, VA, ALU.mult)
                        st.settle()
                    sq = SQ[:, :, :].rearrange("p t (h d) -> p (t h) d", d=P)
                    st.do(v.tensor_reduce(ss[:, 0:16], sq, AX.X, ALU.add))
                    st.settle()
                    inv_mean(rs[:, 0:16], ss[:, 0:16], P, 1e-6, sem("mean_ready"))
                    dve.wait_ge(sem("root_ready"), n + 1)
                    buf = VA if kind == "va" else T2
                    x = buf[:, :, :].rearrange("p t (h d) -> p (t h) d", d=P)
                    tt_(x, x, per(rs[:, 0:16], [P, 16, P]), ALU.mult)
                    st.settle()
                    if kind == "va":
                        tt_(VA, VA, gmg[:, :].unsqueeze(1).to_broadcast([P, TT, 512]), ALU.mult)
                    else:
                        dve.sem_inc(sem("norm_ready"), 1)
                elif kind == "out2":
                    if i == 0:
                        dve.wait_ge(sem("gate_landed"), 16)
                    for tt in range(TT):
                        key = ("P", c, tt)
                        tt_(gtmp, filled(dve, key)[:, :], gate[:, i * 512:(i + 1) * 512], ALU.mult, *freed(key))
                        st.settle()
                        part = H[:, tt, i * 512:(i + 1) * 512]
                        tt_(part, part, gtmp, ALU.add)
                        st.settle()

            def stage(n):
                for c in STAGES[n]:
                    if c in MODSUM:
                        mod_take(MODSUM[c])
                    work(c)
                    mod_hook(c)

            stage(0)
            bar()

            tt_(dtx[:, :, :], SM[:, :, 80:96], dtb[:, :].unsqueeze(1).to_broadcast([P, TT, 16]), ALU.add)
            st.settle()
            ts(dmx[:, :, :], dtx[:, :, :], 0.0, None, ALU.max)
            stt(dna[:, :, :], dtx[:, :, :], -1.0, dtx[:, :, :], ALU.mult, ALU.min, s=sem("dt_in"))
            dve.wait_ge(sem("dt_log"), 1)
            tt_(dt_[:, :, :], dna[:, :, :], dmx[:, :, :], ALU.add)
            st.settle()
            stt(dtA[:, :, :], dt_[:, :, :], -1.0, ea[:, :].unsqueeze(1).to_broadcast([P, TT, 16]), ALU.mult, ALU.mult, s=sem("dtA_ready"))
            bk = filled(dve, "cum")
            st.do(v.tensor_copy(acum[:, :, :].rearrange("p t h -> p (t h)"), bk[:, 0:64]))
            st.do(v.tensor_copy(tot[:, :, :].rearrange("p t h -> p (t h)"), bk[:, 64:128]), *freed("cum"))
            st.settle()
            tt_(dec[:, :, :], tot[:, :, :], acum[:, :, :], ALU.subtract, s=sem("cum_ready"))
            dve.wait_ge(sem("cum_exp"), 1)

            def heads(x, n=64):
                return x.rearrange("p (h e) -> p h e", e=n)

            def front(i):
                c, g = divmod(i, SG)
                if g == 0:
                    if c >= 2:
                        filled(dve, ("Y", 4 * (c - 1) - 1))
                        filled(dve, ("ST", 4 * (c - 1) - 1))
                    tt_(heads(xdt[:, c % 2, :]), heads(xs[:, c, :]), per(dt_[:, c, :], [P, 16, 64]), ALU.mult)
                    st.settle()
                    tt_(heads(xdd[:, c % 2, :]), heads(xdt[:, c % 2, :]), per(dec[:, c, :], [P, 16, 64]), ALU.mult)
                tt_(GT[:, i % 2, :], filled(dve, ("G", i))[:, 0:P], C["upto"], ALU.mult, *freed(("G", i)))
                bk = filled(dve, ("AC", i))
                for r in range(SR):
                    h = 4 * g + r
                    ts(Dm[:, i % 2, r, :], bk[:, r * P:(r + 1) * P], acum[:, c, h:h + 1], 0.0, ALU.subtract, ALU.min,
                       **(dict(zip(("s", "n"), freed(("AC", i)))) if r == SR - 1 else {}))
                st.settle()
                dve.sem_inc(sem("diff_ready"), 1)

            def middle(i):
                dve.wait_ge(sem("diff_exp"), i + 1)
                tt_(Mt[:, i % 2], Dm[:, i % 2], GT[:, i % 2, :].unsqueeze(1).to_broadcast([P, SR, P]), ALU.mult, s=sem("decay_ready"))

            def back(i):
                c, g = divmod(i, SG)
                cols = slice(g * 256, (g + 1) * 256)
                bk = filled(dve, ("Y", i))
                tt_(heads(t2), heads(xs[:, c, cols]), per(dsk[:, 4 * g:4 * g + 4], [P, 4, 64]), ALU.mult)
                st.settle()
                if c:
                    tt_(heads(t1), heads(bk[:, 256:512]), per(eac[:, c, 4 * g:4 * g + 4], [P, 4, 64]), ALU.mult)
                    st.settle()
                    tt_(t2, t2, t1, ALU.add)
                    st.settle()
                tt_(t1, bk[:, 0:256], t2, ALU.add, *freed(("Y", i)))
                st.settle()
                z = Z[:, c, cols]
                tt_(z, z, t1, ALU.mult)
                st.settle()
                st.do(v.tensor_tensor_reduce(out=t1, in0=z, in1=z, scale=1.0, scalar=0.0, op0=ALU.mult, op1=ALU.add,
                                             accum_out=ss[:, i:i + 1]))
                if i < 12:
                    hs = Hst[:, cols]
                    bs = filled(dve, ("ST", i))
                    if c == 0:
                        st.do(v.tensor_copy(hs, bs[:, 0:256]), *freed(("ST", i)))
                    else:
                        tt_(heads(hs), heads(hs), per(cdec[:, c, 4 * g:4 * g + 4], [P, 4, 64]), ALU.mult)
                        st.settle()
                        tt_(hs, hs, bs[:, 0:256], ALU.add, *freed(("ST", i)))
                    st.settle()
                    dve.sem_inc(sem("state_ready"), 1)

            front(0)
            for i in range(16):
                if i < 15:
                    front(i + 1)
                middle(i)
                if i:
                    back(i - 1)
            back(15)
            st.settle()
            inv_mean(rs[:, 0:16], ss[:, 0:16], 256, 1e-5, sem("ms_ready"))
            dve.wait_ge(sem("ms_root"), 1)
            for i in range(16):
                c, g = divmod(i, SG)
                z = Z[:, c, g * 256:(g + 1) * 256]
                ts(z, z, rs[:, i:i + 1], None, ALU.mult, s=sem("gated_ready"))
            bar()
            stage(1)
            bar()

            n_relu = 0
            n_exp = 0
            for i in range(TT):
                nk = (i + 1) * P
                diag = slice(i * P, nk)
                if i == 0:
                    ts(BIAS[:, 0:P], C["late_chunk"], NEG, None, ALU.mult)
                else:
                    sc = SC[:, 0:nk]
                    for hd in range(IH):
                        filled(dve, ("IX", i, hd))
                        dve.wait_ge(freed(("IX", i, hd))[0], freed(("IX", i, hd))[1])
                        n_relu += 1
                        if hd == 0:
                            ts(sc, R[:, hd % 2, 0:nk], wi[:, i, hd:hd + 1], None, ALU.mult, s=sem("relu_used"))
                        else:
                            st.settle()
                            stt(sc, R[:, hd % 2, 0:nk], wi[:, i, hd:hd + 1], sc, ALU.mult, ALU.add, s=sem("relu_used"))
                    st.settle()
                    stt(SC[:, diag], C["late_chunk"], OUT_OF_REACH, SC[:, diag], ALU.mult, ALU.add)
                    for _ in range(TOPK // 8):
                        st.settle()
                        st.do(v.max(m8[:, :], sc))
                        st.settle()
                        st.do(v.match_replace(out=sc, in_to_replace=m8[:, :], in_values=sc, imm_value=TAKEN))
                    st.settle()
                    ts(BIAS[:, 0:nk], sc, -3.35e38, NEG, ALU.is_gt, ALU.mult)
                st.settle()
                for g in range(KVH):
                    if i or g:
                        pi, pg_ = (i, 0) if g else (i - 1, 1)
                        for kb in range(pi + 1):
                            filled(dve, ("PT", pi, pg_, kb))
                    for r in range(4):
                        key = ("S", i, 4 * g + r)
                        bk = filled(dve, key)
                        st.do(v.tensor_tensor_reduce(out=Pb[:, r, 0:nk], in0=bk[:, 0:nk], in1=BIAS[:, 0:nk], scale=float(DH) ** -0.5,
                                                     scalar=-3e38, op0=ALU.add, op1=ALU.max, accum_out=mx[:, r:r + 1]), *freed(key))
                        st.settle()
                        ts(nm[:, r:r + 1], mx[:, r:r + 1], -1.0, None, ALU.mult, s=sem("max_ready"))
                    n_exp += 4
                    dve.wait_ge(sem("exp_done"), n_exp)
                    st.do(v.reciprocal(rc[:, :], sm[:, :]))
                    st.settle()
                    for r in range(4):
                        ts(Pb[:, r, 0:nk], Pb[:, r, 0:nk], rc[:, r:r + 1], None, ALU.mult)
                    st.settle()
                    dve.sem_inc(sem("probs_ready"), 1)
                    key = ("PV", i, g)
                    bk = filled(dve, key)
                    o = M[:, 4 * g:4 * g + 4, i * P:(i + 1) * P]
                    tt_(o, o, bk[:, :].rearrange("p (r q) -> p r q", r=4), ALU.mult, *freed(key))
            bar()
            stage(2)
            bar()

            for tt in range(TT):
                st.do(v.bn_aggr(mv[:, tt, :], bst[:, tt, :, :].rearrange("p c s -> p (c s)")))
            st.settle()
            ts(rs[:, 0:4], mv[:, :, 1], 1e-5, None, ALU.add)
            st.settle()
            st.do(v.reciprocal(rs[:, 0:4], rs[:, 0:4]), sem("var_ready"))
            dve.wait_ge(sem("var_root"), 1)
            dve.wait_ge(sem("ln_landed"), 32)
            for tt in range(TT):
                row = H[:, tt, :]
                ts(row, row, mv[:, tt, 0:1], rs[:, tt:tt + 1], ALU.subtract, ALU.mult)
                st.settle()
                tt_(row, row, lng, ALU.mult)
                st.settle()
                tt_(row, row, lnb, ALU.add, sem("h_rows"))
            stt(G1[:, :], MV[:, 1, :], 1.0, n1g[:, :], ALU.add, ALU.mult)
            st.settle()

            def norm_hidden(n):
                dve.wait_ge(sem("sq_done"), 4 * n + 4)
                inv_mean(rs[:, 0:4], ss[:, 0:4], D, 1e-6, sem("msq_ready"))
                dve.wait_ge(sem("msq_root"), n + 1)
                for tt in range(TT):
                    ts(XN[:, tt, :], H[:, tt, :], rs[:, tt:tt + 1], None, ALU.mult, s=sem("xn_ready"))

            norm_hidden(0)
            for kt in range(0, KD, 2):
                key = ("hT", kt)
                ts(X[:, kt, :], filled(dve, key)[:, :], G1[:, kt:kt + 1], MV[:, 0, kt:kt + 1], ALU.mult, ALU.add, *freed(key))
            bk = filled(dve, "wsT")
            tt_(WS[:, :, :], bk[:, :].rearrange("p (g t) -> p g t", g=4), C["upto"].unsqueeze(1).to_broadcast([P, 4, P]), ALU.mult, *freed("wsT"))
            bar()
            stage(3)
            bar()

            for tt in range(TT):
                key = ("SPG", tt)
                bk = filled(dve, key)
                for g in range(4):
                    cols = slice(g * P, (g + 1) * P)
                    stt(Y[:, tt, cols], bk[:, cols], pack[:, 98 + g:99 + g], UA[:, tt, cols], ALU.add, ALU.mult,
                        *(freed(key) if g == 3 else (None, None)))
            for h in range(4):
                for j in range(4):
                    k = 4 * h + j
                    n = S - P * j
                    z = filled(dve, ("Z", h, j))[:, 0:n]
                    if h and j == 0:
                        dve.wait_ge(sem("log_a_ready"), 4 * h)
                    ts(SPl[j], z, 0.0, None, ALU.max)
                    st.settle()
                    stt(EA[:, k % 2, 0:n], SPl[j], -2.0, z, ALU.mult, ALU.add, s=sem("abs_ready"))
                    dve.wait_ge(sem("log_ready"), k + 1)
                    tt_(SPl[j], SPl[j], EA[:, k % 2, 0:n], ALU.add)
                    st.settle()
                    tt_(SPl[j][:, 0:P], SPl[j][:, 0:P], C["before"], ALU.mult, sem("fail_ready"))
                key = ("O", h)
                bk = filled(dve, key)
                st.do(v.tensor_copy(Y[:, :, 512 + h * P:512 + (h + 1) * P], bk[:, :].rearrange("p (t d) -> p t d", t=TT)), *freed(key))
            st.settle()
            tt_(YSQ, Y, Y, ALU.mult)
            st.settle()
            st.do(v.tensor_reduce(ss[:, 0:32], YSQ[:, :, :].rearrange("p t (h d) -> p (t h) d", d=P), AX.X, ALU.add))
            st.settle()
            inv_mean(rs[:, 0:32], ss[:, 0:32], P, 1e-6, sem("mean_ready"))
            dve.wait_ge(sem("root_ready"), 4)
            x = Y[:, :, :].rearrange("p t (h d) -> p (t h) d", d=P)
            tt_(x, x, per(rs[:, 0:32], [P, 32, P]), ALU.mult, sem("y_ready"))
            bar()
            stage(4)
            bar()
            for tt in range(TT):
                dve.sem_inc(sem("h_rows"), 1)
            stt(G2[:, :], MV[:, 4, :], 1.0, n2g[:, :], ALU.add, ALU.mult)
            st.settle()
            norm_hidden(1)
            for kt in range(0, KD, 2):
                key = ("h2T", kt)
                ts(X[:, kt, :], filled(dve, key)[:, :], G2[:, kt:kt + 1], MV[:, 3, kt:kt + 1], ALU.mult, ALU.add, *freed(key))
            st.settle()
            dve.sem_inc(sem("h2T_dve"), 8)

            bk = filled(dve, "router")
            tt_(L[:, :, :], bk[:, 0:144].rearrange("p (t e) -> p t e", t=TT), br[:, :].unsqueeze(1).to_broadcast([P, TT, 36]), ALU.add, *freed("router"))
            st.settle()
            gl = L[:, :, 0:4]
            st.do(v.tensor_reduce(gm1[:, :], gl, AX.X, ALU.max))
            st.settle()
            tt_(r4[:, :, :], gl, per(gm1[:, :], [P, TT, 4]), ALU.subtract)
            tt_(oh[:, :, :], gl, per(gm1[:, :], [P, TT, 4]), ALU.is_equal, sem("group_in"))

            def first_of(onehot, scratch_max, width):
                rank = C["rank4" if width == 4 else "rank8"].unsqueeze(1).to_broadcast([P, TT, width])
                st.settle()
                tt_(onehot, onehot, rank, ALU.mult)
                st.settle()
                st.do(v.tensor_reduce(scratch_max, onehot, AX.X, ALU.max))
                st.settle()
                tt_(onehot, onehot, per(scratch_max, [P, TT, width]), ALU.is_equal)
                st.settle()

            first_of(oh[:, :, :], tmx[:, :], 4)
            dve.wait_ge(sem("group_exp"), 1)
            st.do(v.tensor_reduce(pg[:, :], r4[:, :, :], AX.X, ALU.add))
            st.settle()
            st.do(v.reciprocal(pg[:, :], pg[:, :]))
            for g in range(NG):
                tt_(el3[:, :, g, :], L[:, :, 4 + 8 * g:12 + 8 * g], oh[:, :, g:g + 1].to_broadcast([P, TT, 8]), ALU.mult)
            st.settle()
            st.do(v.tensor_reduce(el[:, :, :], el3[:, :, :, :].rearrange("p t g j -> p t j g"), AX.X, ALU.add))
            st.settle()
            st.do(v.tensor_reduce(e1v[:, :], el[:, :, :], AX.X, ALU.max))
            st.settle()
            tt_(o1[:, :, :], el[:, :, :], per(e1v[:, :], [P, TT, 8]), ALU.is_equal)
            first_of(o1[:, :, :], tmx[:, :], 8)
            stt(el[:, :, :], o1[:, :, :], OUT_OF_REACH, el[:, :, :], ALU.mult, ALU.add)
            st.settle()
            st.do(v.tensor_reduce(e2v[:, :], el[:, :, :], AX.X, ALU.max))
            st.settle()
            tt_(o2[:, :, :], el[:, :, :], per(e2v[:, :], [P, TT, 8]), ALU.is_equal)
            first_of(o2[:, :, :], tmx[:, :], 8)
            tt_(e2v[:, :], e2v[:, :], e1v[:, :], ALU.subtract, sem("pair_in"))
            for E, o in ((E1, o1), (E2, o2)):
                for g in range(NG):
                    tt_(E[:, :, 8 * g:8 * g + 8], o[:, :, :], oh[:, :, g:g + 1].to_broadcast([P, TT, 8]), ALU.mult)
            st.settle()
            tt_(EM[:, :, :], E1[:, :, :], E2[:, :, :], ALU.add, sem("choice_ready"))
            dve.wait_ge(sem("pair_exp"), 1)
            ts(wa[:, :], e2v[:, :], 1.0, None, ALU.add)
            st.settle()
            st.do(v.reciprocal(wa[:, :], wa[:, :]))
            st.settle()
            tt_(wa[:, :], wa[:, :], pg[:, :], ALU.mult)
            st.settle()
            tt_(wb[:, :], wa[:, :], e2v[:, :], ALU.mult)
            bk = filled(dve, "rank")
            cnt = RA[:, 0:256].rearrange("p (e k) -> p e k", k=8)
            st.do(v.tensor_copy(nbk[:, :], bk[:, P:P + NE]))
            st.settle()
            tt_(cnt, per(nbk[:, :], [P, NE, 8]), C["thresholds"].unsqueeze(1).to_broadcast([P, NE, 8]), ALU.is_gt)
            st.settle()
            st.do(v.tensor_reduce(nbk[:, :], cnt, AX.X, ALU.add))
            st.settle()
            st.do(v.tensor_tensor_scan(bend[:, :], C["ones"][:, 0:NE], nbk[:, :], 0.0, ALU.mult, ALU.add))
            st.settle()
            tt_(nbk[:, :], bend[:, :], nbk[:, :], ALU.subtract)
            st.settle()
            stt(slot[:, :, :], nbk[:, :].unsqueeze(1).to_broadcast([P, TT, NE]), float(BLK), bk[:, 0:P].rearrange("p (t e) -> p t e", t=TT),
                ALU.mult, ALU.add, *freed("rank"))
            st.settle()
            for k, E in enumerate((E1, E2)):
                tt_(E[:, :, :], E[:, :, :], slot[:, :, :], ALU.mult)
                st.settle()
                st.do(v.tensor_reduce(sl[:, k, :], E[:, :, :], AX.X, ALU.add))
            st.settle()
            st.do(v.tensor_copy(sli[:, :, :], sl[:, :, :]))
            st.do(v.tensor_copy(toki[:, :], C["tokens"]))
            wide = RA[0:1, 256:256 + NBLK * NE].rearrange("p (b e) -> p b e", e=NE)
            tt_(wide, bend[0:1, :].unsqueeze(1).to_broadcast([1, NBLK, NE]), per(C["block_no"][0:1, :], [1, NBLK, NE]), ALU.is_le)
            st.settle()
            st.do(v.tensor_reduce(blke[:, :], wide, AX.X, ALU.add))
            st.settle()
            ts(blke[:, :], blke[:, :], NE - 1.0, None, ALU.min)
            st.settle()
            st.do(v.tensor_copy(blki[:, :], blke[:, :]))
            st.do(v.tensor_copy(nbi[:, :], bend[0:1, NE - 1:NE]))
            st.settle()
            dve.sem_inc(sem("routed"), 1)
            bar()
            blocks = dve.value_load(nbi[0:1, 0:1], min_val=1, max_val=NBLK)
            with dve.Fori(0, NBLK // 2) as i:
                with dve.If(i * 2 < blocks):
                    for u in range(2):
                        dve.wait_ge(sem(f"t_done{u}"), i + 1)
                        dve.wait_ge(sem(f"up_done{u}"), i)
                        for n in range(2):
                            half = slice(8 * n, 8 * n + 8)
                            ins = v.tensor_tensor(xmul[:, half, :], ps[n][:, :].rearrange("p (k s) -> p k s", s=BLK),
                                                  per(G2[:, half], [P, 8, BLK]), ALU.mult)
                        ins.then_inc(sem("t_taken"), 1)
                        dve.wait_ge(sem("t_taken"), i * 2 + u + 1)
                        v.tensor_tensor(xgT[u], xmul, per(MV[:, 3, :], [P, KD, BLK]), ALU.add).then_inc(sem("xt_ready"), 1)
                        dve.wait_ge(sem("silu_gate"), i * 2 + u + 1)
                        v.tensor_tensor(hb[u], SGt[u].rearrange("p (m s) -> p m s", m=2), ps[3][:, 0:P].rearrange("p (m s) -> p m s", m=2),
                                        ALU.mult).then_inc(sem("h_ready"), 1)
                        dve.wait_ge(sem(f"down_done{u}"), i + 1)
                        dve.wait_ge(sem(f"y_stored{u}"), i * 16)
                        v.tensor_copy(yb[u][:, 0:512], ps[4][0:BLK, :])
                        v.tensor_copy(yb[u][:, 512:1024], ps[5][0:BLK, :]).then_inc(sem("y_taken_dve"), 1)
            dve.sem_inc(phase["dve"], 1)
            dve.wait_ge(sem("gate_landed"), 32)
            for tt in range(TT):
                y0, y1 = picked[tt % 2]
                dve.wait_ge(sem(f"picked_landed{tt % 2}"), 32 * (tt // 2 + 1))
                ts(y0, y0, wa[:, tt:tt + 1], None, ALU.mult)
                st.settle()
                stt(y0, y1, wb[:, tt:tt + 1], y0, ALU.mult, ALU.add)
                st.settle()
                tt_(y0, y0, gate, ALU.mult)
                st.settle()
                tt_(H[:, tt, :], H[:, tt, :], y0, ALU.add, sem("out_ready"))
                st.settle()
                dve.sem_inc(sem("picked_used"), 1)


_INS = ["x", "w_in", "w_out", "conv_w", "conv_b", "dt_bias", "a_log", "d_skip", "ssd_norm_w", "ln_g", "ln_b", "c_2",
        "w_mod_2", "b_mod_2", "mod_layer_2", "norm1_g_2", "w_in_2", "gm_norm_g_2", "gm_ws_2", "gm_bs_2", "q_norm_g_2",
        "k_norm_g_2", "out_norm_g_2", "w_out_2", "norm2_g_2", "w_group_2", "b_group_2", "w_route_2", "b_route_2",
        "w_gate_2", "w_up_2", "w_down_2"]


def kernel(**inputs):
    import concourse.bacc as bacc
    from concourse.bass_utils import run_bass_kernel_spmd as run

    nc = bacc.Bacc("TRN2", target_bir_lowering=False, num_devices=1)
    arrays, args = {}, {}
    for name in _INS:
        arr = np.ascontiguousarray(inputs[name])
        arrays[f"in_{name}"] = arr
        args[name] = nc.dram_tensor(f"in_{name}", arr.shape, mybir.dt.from_np(arr.dtype), kind="ExternalInput").ap()
    arrays["in_const"] = CONST
    args["const"] = nc.dram_tensor("in_const", CONST.shape, F32, kind="ExternalInput").ap()
    out = nc.dram_tensor("out_0", (1, S, D), F32, kind="ExternalOutput").ap()
    program(nc, args, out)
    r = run(nc, [arrays], core_ids=[0])
    return r.results[0]["out_0"]
```

```python
import concourse.bass as bass
from concourse import mybir
from contextlib import ExitStack
import numpy as np

F32 = mybir.dt.float32
I32 = mybir.dt.int32
ALU = mybir.AluOpType
ACT = mybir.ActivationFunctionType
AX = mybir.AxisListType

P = 128
S = 512
D = 2048
TT = S // P
KD = D // P
BLK = 64
NE, NG, EPG, DE = 32, 4, 8, 256
NBLK = 48
QH, KVH, DH = 8, 2, 128
IH, ID = 16, 64
TOPK = 128
SG, SR, SP_ = 4, 4, 64
ALPHA = 2.0 ** 0.25
NEG = -1e30
OUT_OF_REACH = -3.3e38
TAKEN = -3.4e38

C_Q, C_K, C_ZA, C_QI, C_KI, C_Z, C_XBC, C_DT = 0, 1024, 1536, 2560, 3584, 3664, 4688, 6736


def host_constants():
    p = np.arange(P)[:, None]
    f = np.arange(P)[None, :]
    tok = (np.arange(TT)[None, :] * P + p).astype(np.float32)

    def rope(rot, theta=500000.0):
        half = rot // 2
        inv = np.float32(theta) ** (-np.arange(half, dtype=np.float32) * np.float32(2.0) / np.float32(rot))
        ang = (tok[:, :, None] * inv.astype(np.float32)[None, None, :]).astype(np.float32)
        c, s = np.cos(ang.astype(np.float64)), np.sin(ang.astype(np.float64))
        return (np.concatenate([c, c], -1).reshape(P, -1), np.concatenate([s, -s], -1).reshape(P, -1))

    cos_a, sin_a = rope(DH // 4)
    cos_i, sin_i = rope(ID // 4)
    parts = {
        "ident": (p == f),
        "upto": (p <= f),
        "before": (p < f),
        "not_before": np.where(p >= f, NEG, 0.0),
        "neg_from": -(p >= f).astype(np.float32),
        "neg_ones": -np.ones((P, P)),
        "ones": np.ones((P, P)),
        "late_chunk": ((p < 64) & (f >= 64)),
        "cos_a": cos_a, "sin_a": sin_a, "cos_i": cos_i, "sin_i": sin_i,
        "thresholds": np.broadcast_to((np.arange(8) * BLK).astype(np.float32)[None, :], (P, 8)),
        "block_no": np.broadcast_to(np.arange(NBLK, dtype=np.float32)[None, :], (P, NBLK)),
        "rank4": np.broadcast_to((4.0 - np.arange(4))[None, :], (P, 4)),
        "rank8": np.broadcast_to((8.0 - np.arange(8))[None, :], (P, 8)),
        "tokens": tok,
    }
    at, cols, out = 0, {}, []
    for name, a in parts.items():
        a = np.ascontiguousarray(a).astype(np.float32)
        cols[name] = (at, at + a.shape[1])
        at += a.shape[1]
        out.append(a)
    return np.concatenate(out, 1), cols


CONST, COLS = host_constants()


class Steps:

    def __init__(self, eng, own):
        self.eng, self.own, self.n, self.last, self.counts = eng, own, 0, None, {}

    def do(self, ins, sem=None, value=None):
        if sem is None:
            self.n += 1
            ins.then_inc(self.own, 1)
            self.last = (self.own, self.n)
        else:
            if value is None:
                value = self.counts[sem.name] = self.counts.get(sem.name, 0) + 1
            ins.then_inc(sem, 1)
            self.last = (sem, value)

    def settle(self):
        self.eng.wait_ge(*self.last)


def program(nc, a, out):
    ctx = ExitStack()
    with ctx:
        def sb(name, shape, dt=F32):
            return ctx.enter_context(nc.sbuf_tensor(name, shape, dt))

        sems = {}

        def sem(name):
            if name not in sems:
                sems[name] = ctx.enter_context(nc.semaphore(name))
            return sems[name]

        RX = sb("RX", [P, 8192])
        RH = sb("RH", [P, 8192])
        RM = sb("RM", [P, 8192])
        RW = sb("RW", [P, 8192])
        RA = sb("RA", [P, 10240])
        RG = sb("RG", [P, 6144])
        cst = sb("cst", [P, CONST.shape[1]])
        C = {k: cst[:, i:j] for k, (i, j) in COLS.items()}
        ident = C["ident"]
        ps = [ctx.enter_context(nc.psum_tensor(f"bank{i}", [P, 512], F32)) for i in range(8)]

        X = RX[:, :].rearrange("p (k t) -> p k t", k=KD)
        H = RH[:, :].rearrange("p (t d) -> p t d", t=TT)
        Hx = RH[:, :].rearrange("p (t q k) -> p t k q", t=TT, k=KD)
        M = RM[:, :].rearrange("p (k t) -> p k t", k=KD)
        W = RW[:, :].rearrange("p (s k n) -> p s k n", s=4, k=4)
        macc = RG[:, 0:2048]
        mring = RG[:, 2048:6144].rearrange("p (s n) -> p s n", s=2)
        xs = RH[:, 0:4096].rearrange("p (t e) -> p t e", t=TT)
        bfm = RH[:, 4096:6144].rearrange("p (g t) -> p g t", g=SG)
        cfm = RH[:, 6144:8192].rearrange("p (g t) -> p g t", g=SG)
        btm = RA[:, 0:2048].rearrange("p (t e) -> p t e", t=TT)
        SL = RA[:, 2048:4096].rearrange("p (s t) -> p s t", s=4)
        CV = RA[:, 4096:5120].rearrange("p (s t) -> p s t", s=2)
        xdt = RA[:, 2048:4096].rearrange("p (s e) -> p s e", s=2)
        xdd = RA[:, 4096:6144].rearrange("p (s e) -> p s e", s=2)
        Hst = RA[:, 6144:7168]
        Dm = RA[:, 7168:8192].rearrange("p (s r l) -> p s r l", s=2, r=SR)
        Mt = RA[:, 8192:9216].rearrange("p (s r l) -> p s r l", s=2, r=SR)
        neg_ident = RA[:, 9216:9344]
        t1 = RA[:, 9472:9728]
        sqj = RA[:, 9728:9984]
        Z = RM[:, 0:4096].rearrange("p (t e) -> p t e", t=TT)
        qT = RH[:, 0:4096].rearrange("p (h t) -> p h t", h=QH)
        qiT = RH[:, 4096:8192].rearrange("p (h t) -> p h t", h=QH)
        kT = RA[:, 0:1024].rearrange("p (h t) -> p h t", h=KVH)
        kiT = sb("kiT", [P, S])[:, :]
        V = RA[:, 1536:2560].rearrange("p (t e) -> p t e", t=TT)
        BIAS = [RA[:, 3072:3200], RA[:, 3200:3456], RA[:, 9216:9600], RA[:, 2560:3072]]
        R = [RA[:, b:b + 512] for b in (3584, 4096, 7680, 8192)]
        Pb = [x.rearrange("p (h n) -> p h n", h=4) for x in (RA[:, 4608:6656], RX[:, 2048:4096])]
        T = RA[:, 4608:6656].rearrange("p (t n) -> p t n", t=TT)
        PT = [x.rearrange("p (k n) -> p k n", k=4) for x in (RA[:, 6656:8704], RX[:, 4096:6144])]
        RT = RA[:, 6656:7680].rearrange("p (s n) -> p s n", s=2)
        TK = RA[:, 8704:9216].rearrange("p (t n) -> p t n", t=TT)
        lng = RA[:, 0:2048]
        lnb = RA[:, 2048:4096]
        junk = RA[:, 4096:6144]
        XN = RM[:, :].rearrange("p (t d) -> p t d", t=TT)
        XNx = RM[:, :].rearrange("p (t q k) -> p t k q", t=TT, k=KD)
        VA = RA[:, 0:2048].rearrange("p (t e) -> p t e", t=TT)
        UA = RA[:, 2048:4096].rearrange("p (t e) -> p t e", t=TT)
        T2 = RA[:, 4096:6144].rearrange("p (t e) -> p t e", t=TT)
        V2 = RA[:, 6144:8192].rearrange("p (t e) -> p t e", t=TT)
        SQ = RA[:, 8192:10240].rearrange("p (t e) -> p t e", t=TT)
        qT2 = RM[:, 0:2048].rearrange("p (h t) -> p h t", h=4)
        kT2 = RM[:, 2048:4096].rearrange("p (h t) -> p h t", h=4)
        Y = RM[:, 4096:8192].rearrange("p (t e) -> p t e", t=TT)
        yT = RX[:, 0:4096].rearrange("p (k t) -> p k t", k=8)
        off = [0, 512, 896, 1152]
        TRI = 1280
        SPall, ATall, EAall = ([RX[:, b + TRI * w:b + TRI * (w + 1)] for w in range(2)] for b in (0, 2 * TRI, 4 * TRI))

        def tri(part, j):
            return part[:, off[j]:off[j] + S - P * j]

        YSQ = RX[:, 4096:8192].rearrange("p (t e) -> p t e", t=TT)
        gate = RA[:, 0:2048]
        gate2 = RA[:, 7680:9728]
        gtmp = RA[:, 2048:2560]
        WGt = [RX[:, 4096 * u:4096 * (u + 1)].rearrange("p (k n) -> p k n", k=KD) for u in range(2)]
        WUt = [RM[:, 4096 * u:4096 * (u + 1)].rearrange("p (k n) -> p k n", k=KD) for u in range(2)]
        WDt = [RW[:, 4096 * u:4096 * (u + 1)].rearrange("p (m n) -> p m n", m=2) for u in range(2)]
        xg = [RG[0:BLK, 2048 * u:2048 * (u + 1)] for u in range(2)]
        xgx = [RG[0:BLK, 2048 * u:2048 * (u + 1)].rearrange("p (q k) -> p k q", k=KD) for u in range(2)]
        xgT = [RG[:, 4096 + 1024 * u:4096 + 1024 * (u + 1)].rearrange("p (k s) -> p k s", k=KD) for u in range(2)]
        yb = [RA[0:BLK, 2048 * u:2048 * (u + 1)] for u in range(2)]
        xmul = RA[:, 4096:5120].rearrange("p (k s) -> p k s", k=KD)
        SGt = [RA[:, 5120 + 128 * u:5248 + 128 * u] for u in range(2)]
        hb = [RA[:, 5376 + 128 * u:5504 + 128 * u].rearrange("p (m s) -> p m s", m=2) for u in range(2)]
        picked = [[RX[:, 4096 * u + 2048 * k:4096 * u + 2048 * (k + 1)] for k in range(2)] for u in range(2)]

        SM = sb("SM", [P, TT, 96])
        dtb = sb("dtb", [P, 16])
        alog = sb("alog", [P, 16])
        dsk = sb("dsk", [P, 16])
        convw = sb("convw", [P, 64])
        packrow = sb("packrow", [108, P])
        pack = sb("pack", [P, 108])
        dtx = RA[:, 9984:10048].rearrange("p (t h) -> p t h", t=TT)
        dmx = RA[:, 10048:10112].rearrange("p (t h) -> p t h", t=TT)
        dna = RA[:, 10112:10176].rearrange("p (t h) -> p t h", t=TT)
        dt_ = sb("dt_", [P, TT, 16])
        dtA = sb("dtA", [P, TT, 16])
        ea = alog
        nacum = sb("nacum", [P, TT, 16])
        tot = sb("tot", [P, TT, 16])
        dec = sb("dec", [P, TT, 16])
        eac = sb("eac", [P, TT, 16])
        cdec = sb("cdec", [P, TT, 16])
        ss = sb("ss", [P, 32])
        rs = sb("rs", [P, 32])
        wi = sb("wi", [P, TT, 16])
        m8 = sb("m8", [P, TT, 8])
        mx = sb("mx", [P, 2, 4])
        nm = sb("nm", [P, 2, 4])
        sm = sb("sm", [P, 2, 4])
        rc = sb("rc", [P, 2, 4])
        ccol = sb("ccol", [P, KD])
        csil = ccol
        MV = sb("MV", [P, 6, KD])
        bmod = sb("bmod", [P, 6, KD])
        lmod = sb("lmod", [P, 6, KD])
        n1g = sb("n1g", [P, KD])
        n2g = sb("n2g", [P, KD])
        G1 = sb("G1", [P, KD])
        G2 = sb("G2", [P, KD])
        bst = RA[:, 6144:6240].rearrange("p (t c s) -> p t c s", t=TT, c=4)
        mv = sb("mv", [P, TT, 2])
        gmg = RG[:, 2048:2560]
        WS = RG[:, 2560:3072].rearrange("p (g t) -> p g t", g=4)
        WR = RG[:, 3072:3648].rearrange("p (k e) -> p k e", k=KD)
        br = sb("br", [P, 36])
        L = RA[:, 6144:6288].rearrange("p (t e) -> p t e", t=TT)
        r4 = RA[:, 7168:7184].rearrange("p (t g) -> p t g", g=4)
        oh = RA[:, 7184:7200].rearrange("p (t g) -> p t g", g=4)
        gm1 = sb("gm1", [P, TT])
        pg = sb("pg", [P, TT])
        el3 = RA[:, 6288:6416].rearrange("p (t g e) -> p t g e", t=TT, g=4)
        el = RA[:, 6416:6448].rearrange("p (t e) -> p t e", t=TT)
        o1 = RA[:, 6448:6480].rearrange("p (t e) -> p t e", t=TT)
        o2 = RA[:, 6480:6512].rearrange("p (t e) -> p t e", t=TT)
        tmx = sb("tmx", [P, TT])
        e1v = sb("e1v", [P, TT])
        e2v = sb("e2v", [P, TT])
        wa = sb("wa", [P, TT])
        wb = sb("wb", [P, TT])
        E1 = RA[:, 6512:6640].rearrange("p (t e) -> p t e", t=TT)
        E2 = RA[:, 6640:6768].rearrange("p (t e) -> p t e", t=TT)
        EM = RA[:, 6768:6896].rearrange("p (t e) -> p t e", t=TT)
        nbk = sb("nbk", [P, NE])
        bend = sb("bend", [P, NE])
        slot = RA[:, 6896:7024].rearrange("p (t e) -> p t e", t=TT)
        sl = sb("sl", [P, 2, TT])
        sli = sb("sli", [P, 2, TT], I32)
        toki = sb("toki", [P, TT], I32)
        blke = RA[0:1, 1792:1840]
        blki = sb("blki", [1, NBLK], I32)
        nbi = sb("nbi", [1, 1], I32)
        zidx = RM[:, 2048:2048 + (NBLK + 2) * BLK // P].bitcast(I32)
        IDX = [sb(f"IDX{u}", [BLK, 1], I32) for u in range(2)]

        gates_d = nc.dram_tensor("gates_d", (2, D), F32, kind="Internal").ap()
        xn2_d = nc.dram_tensor("xn2_d", (S, D), F32, kind="Internal").ap()
        slot_d = nc.dram_tensor("slot_d", ((NBLK + 2) * BLK, 1), I32, kind="Internal").ap()
        ys_d = nc.dram_tensor("ys_d", (NBLK * BLK, D), F32, kind="Internal").ap()

        w_in, w_out, w_in2, w_out2 = a["w_in"][0], a["w_out"][0], a["w_in_2"][0], a["w_out_2"][0]
        chunks = [("xbc", w_in, C_XBC + 512 * i, 512, 16, False) for i in range(4)]
        chunks += [("small", w_in, None, 96, 16, True)]
        chunks += [("z", w_in, C_Z + 512 * i, 512, 16, True) for i in range(2)]
        chunks += [("qi", w_in, C_QI + 512 * i, 512, 16, True) for i in range(2)]
        chunks += [("q", w_in, C_Q + 512 * i, 512, 16, True) for i in range(2)]
        chunks += [("kv", w_in, C_K, 512, 16, True)]
        chunks += [("za", w_in, C_ZA + 512 * i, 512, 16, False) for i in range(2)]
        chunks += [("out", w_out, 512 * i, 512, 16, True) for i in range(4)]
        chunks += [(k, w_in2, c, 512, 16, True) for k, c in (("va", 512), ("ua", 0), ("q2", 1024), ("k2", 1536), ("v2", 2048))]
        chunks += [("out2", w_out2, 512 * i, 512, 8, True) for i in range(4)]
        first = {}
        for n, ch in enumerate(chunks):
            first.setdefault(ch[0], n)

        loads, load_of = [], {}
        landed = [0, 0, 0, 0]
        for c, ch in enumerate(chunks):
            for q in range(ch[4] // 4):
                n = len(loads)
                landed[n % 4] += 32 if ch[0] == "small" else 16
                load_of[c, q] = (n % 4, landed[n % 4])
                loads.append((c, q))

        use, times = {}, [0] * 8

        def plan(key, b):
            use[key] = (b, times[b])
            times[b] += 1

        aux = [0]

        def plan_aux(key):
            plan(key, 4 + aux[0] % 4)
            aux[0] += 1

        def posts(c):
            kind = chunks[c][0]
            i = c - first[kind]
            if kind == "xbc":
                return [("T", c, j) for j in range(4)] if i < 3 else []
            if kind == "small":
                return [("T", c, 0)]
            if kind in ("q", "qi", "q2", "k2"):
                return [("T", c, j) for j in range(4)]
            if kind == "kv":
                return [("T", c, j) for j in range(2)]
            return []

        MODSUM = {3 * (v + 1): v for v in range(6)}
        STAGES = [list(range(0, 7)), list(range(7, 14)), list(range(14, 18)), list(range(18, 23)), list(range(23, 27))]
        CUM_AT = first["small"] + 1
        IX_AT = first["q"]
        IX = [(hd, i) for hd in range(IH) for i in range(1, TT)]
        GROUPS = [(i, g) for i in range(TT) for g in range(KVH)]
        for kt in range(KD):
            plan_aux(("xT", kt))
        plan_aux("pack")
        for n, stage in enumerate(STAGES):
            for c in stage:
                for j in range(4):
                    plan(("P", c, j), j)
                if c in MODSUM:
                    plan_aux(("mod", MODSUM[c]))
                if c > stage[0]:
                    for k in posts(c - 1):
                        plan_aux(k)
                if c == CUM_AT:
                    plan_aux("cum")
                if c == IX_AT:
                    for hd, i in IX:
                        plan_aux(("IX", i, hd))
            for k in posts(stage[-1]):
                plan_aux(k)
            if n == 0:
                for i in range(16):
                    plan(("G", i), i % 2)
                    plan(("AC", i), 2 + i % 2)
                    plan(("Y", i), 4 + i % 2)
                    if i < 12:
                        plan(("ST", i), 6 + i % 2)
                for ct in range(8):
                    plan_aux(("ZT", ct))
            if n == 1:
                for i in range(TT):
                    for g in range(KVH):
                        for r in range(4):
                            plan(("S", i, 4 * g + r), r)
                        for kb in range(i + 1):
                            plan(("PT", i, g, kb), 4 + kb % 3)
                        plan(("PV", i, g), 7)
            if n == 2:
                for kt in range(KD):
                    plan_aux(("hT", kt))
                plan_aux("wsT")
            if n == 3:
                for tt in range(TT):
                    plan_aux(("SPG", tt))
                for h in range(4):
                    for j in range(4):
                        plan(("Z", h, j), 4 * (h % 2) + j)
                    plan(("O", h), 4 * (h % 2) + 3)
                for ct in range(8):
                    plan_aux(("yT", ct))
            if n == 4:
                for kt in range(KD):
                    plan_aux(("h2T", kt))
                plan_aux("router")
                plan_aux("rank")

        bank_full = [sem(f"bank_full{i}") for i in range(8)]
        bank_free = [sem(f"bank_free{i}") for i in range(8)]

        def filled(eng, key):
            b, n = use[key]
            eng.wait_ge(bank_full[b], n + 1)
            return ps[b]

        def freed(key):
            b, n = use[key]
            return bank_free[b], n + 1

        phase = {k: sem("phase_" + k) for k in ("pe", "act", "dve", "pool", "sp")}
        phases = {k: 0 for k in phase}

        def barrier(eng, me, who=("pe", "act", "dve")):
            eng.sem_inc(phase[me], 1)
            phases[me] += 1
            for o in who:
                if o != me:
                    eng.wait_ge(phase[o], phases[me])

        small_landed = sem("small_landed")
        x_landed = sem("x_landed")
        slot_free = sem("slot_free")
        w_landed = [sem(f"w_landed{i}") for i in range(4)]
        mod_landed = [sem("mod_landed0"), sem("mod_landed1")]
        mod_used = sem("mod_used")
        mod_ready = sem("mod_ready")
        xT_dve, xT_act = sem("xT_dve"), sem("xT_act")
        SMALL = []
        N_SMALL = 17
        PH_MOE = 10

        block = ctx.enter_context(nc.Block())

        def bcast_row(row):
            return row.partition_broadcast(P)

        @block.sync
        def _(sp):
            ws = a["conv_w"][0].rearrange("t (j p) -> (t j) p", p=P)
            SMALL.append((cst[:, :], a["const"]))
            SMALL.append((ccol[:, :], a["c_2"].rearrange("b (p k) -> (b p) k", k=KD)))
            SMALL.append((packrow[0:64, :], ws))
            SMALL.append((packrow[64:80, :], a["conv_b"].rearrange("l (j p) -> (l j) p", p=P)))
            SMALL.append((packrow[80:88, :], a["ssd_norm_w"].rearrange("l (j p) -> (l j) p", p=P)))
            SMALL.append((packrow[88:96, :], a["out_norm_g_2"].rearrange("l (j p) -> (l j) p", p=P)))
            SMALL.append((packrow[96:97, :], a["q_norm_g_2"]))
            SMALL.append((packrow[97:98, :], a["k_norm_g_2"]))
            SMALL.append((packrow[98:102, :], a["gm_bs_2"][0]))
            SMALL.append((dtb[:, :], bcast_row(a["dt_bias"][0])))
            SMALL.append((alog[:, :], bcast_row(a["a_log"][0])))
            SMALL.append((dsk[:, :], bcast_row(a["d_skip"][0])))
            SMALL.append((bmod[:, :, :], a["b_mod_2"].rearrange("(v p k) -> p v k", v=6, k=KD)))
            SMALL.append((lmod[:, :, :], a["mod_layer_2"][0].rearrange("(v p k) -> p v k", v=6, k=KD)))
            SMALL.append((n1g[:, :], a["norm1_g_2"][0].rearrange("(p k) -> p k", k=KD)))
            SMALL.append((n2g[:, :], a["norm2_g_2"][0].rearrange("(p k) -> p k", k=KD)))
            SMALL.append((br[:, 0:4], bcast_row(a["b_group_2"][0])))
            SMALL.append((br[:, 4:36], bcast_row(a["b_route_2"][0])))
            sp.dma_start(*SMALL[0]).then_inc(sem("const_landed"), 16)
            n = 0
            for c, q in loads:
                kind, w, col, width, kk, _ = chunks[c]
                if n >= 4:
                    sp.wait_ge(slot_free, n - 3)
                if kk == 16 and w.tensor.name != a["w_out"].tensor.name:
                    rows = w.rearrange("(p k) n -> p k n", k=KD)
                else:
                    rows = w.rearrange("(k p) n -> p k n", p=P)
                if kind == "small":
                    sp.dma_start(W[:, n % 4, :, 0:80], rows[:, 4 * q:4 * q + 4, C_KI:C_KI + 80]).then_inc(w_landed[n % 4], 16)
                    sp.dma_start(W[:, n % 4, :, 80:96], rows[:, 4 * q:4 * q + 4, C_DT:C_DT + 16]).then_inc(w_landed[n % 4], 16)
                else:
                    sp.dma_start(W[:, n % 4, :, :], rows[:, 4 * q:4 * q + 4, col:col + 512]).then_inc(w_landed[n % 4], 16)
                n += 1
                if n == 4:
                    for dst, src in SMALL[1:]:
                        sp.dma_start(dst, src).then_inc(small_landed, 16)
            sp.wait_ge(sem("routed"), 1)
            for me in ("pe", "act", "dve"):
                sp.wait_ge(phase[me], PH_MOE)
            blocks = sp.value_load(nbi[0:1, 0:1], min_val=1, max_val=NBLK)
            wgv = a["w_gate_2"][0].rearrange("e (p k) n -> e p k n", k=KD)
            wuv = a["w_up_2"][0].rearrange("e (p k) n -> e p k n", k=KD)
            wdv = a["w_down_2"][0].rearrange("e (m p) n -> e p m n", p=P)
            with sp.Fori(0, NBLK // 2) as i:
                with sp.If(i * 2 < blocks):
                    for u in range(2):
                        e = sp.value_load(blki[0:1, bass.ds(i * 2 + u, 1)], min_val=0, max_val=NE - 1)
                        sp.wait_ge(sem(f"up_done{u}"), i + 1)
                        sp.dma_start(WGt[u], wgv[e]).then_inc(sem(f"wg_landed{u}"), 16)
                        sp.dma_start(WUt[u], wuv[e]).then_inc(sem(f"wu_landed{u}"), 16)
                        sp.wait_ge(sem(f"down_done{u}"), i + 1)
                        sp.dma_start(WDt[u], wdv[e]).then_inc(sem(f"wd_landed{u}"), 16)

        @block.gpsimd
        def _(pool):
            st = Steps(pool, sem("pool_done"))
            st.do(nc.gpsimd.memset(zidx[:, :], 0))
            st.settle()
            pool.dma_start(slot_d.rearrange("(p n) o -> p (n o)", p=P), zidx[:, :]).then_inc(sem("idx_cleared"), 16)
            wm = a["w_mod_2"].rearrange("(p k) n -> p k n", k=KD)
            for s in range(6 * KD):
                v, kt = divmod(s, KD)
                if s == 40:
                    for me in ("pe", "act", "dve"):
                        pool.wait_ge(phase[me], 1)
                    pool.wait_ge(small_landed, 16 * N_SMALL)
                    pool.wait_ge(sem("dtA_ready"), 1)
                    pool.wait_ge(sem("cum_exp"), 1)
                    for c in range(TT):
                        def heads(x):
                            return x.rearrange("p (h e) -> p h e", e=64)

                        def per_head(x):
                            return x.unsqueeze(2).to_broadcast([P, 16, 64])

                        if c >= 2:
                            filled(pool, ("Y", 4 * (c - 1) - 1))
                            filled(pool, ("ST", 4 * (c - 1) - 1))
                        st.do(nc.gpsimd.tensor_tensor(heads(xdt[:, c % 2, :]), heads(xs[:, c, :]), per_head(dt_[:, c, :]), ALU.mult))
                        st.settle()
                        st.do(nc.gpsimd.tensor_tensor(heads(xdd[:, c % 2, :]), heads(xdt[:, c % 2, :]), per_head(dec[:, c, :]), ALU.mult),
                              sem("xd_ready"))
                        st.do(nc.gpsimd.tensor_tensor(heads(xs[:, c, :]), heads(xs[:, c, :]), per_head(dsk[:, :]), ALU.mult), sem("skip_ready"))
                if s >= 2:
                    pool.wait_ge(mod_used, s - 1)
                if s == 75:
                    for me in ("pe", "act", "dve"):
                        pool.wait_ge(phase[me], 3)
                    st.do(nc.gpsimd.memset(RX[:, 0:D], 0.0))
                    st.settle()
                    spare = ys_d[16 * BLK:, :].rearrange("(n p) d -> p n d", p=P)
                    pool.dma_start(spare, RX[:, 0:D].unsqueeze(1).to_broadcast([P, (NBLK - 16) * BLK // P, D])).then_inc(sem("ys_cleared"), 16)
                pool.dma_start(mring[:, s % 2, :], wm[:, kt, v * D:(v + 1) * D]).then_inc(mod_landed[s % 2], 16)
            pool.wait_ge(sem("routed"), 1)
            pool.wait_ge(sem("idx_cleared"), 16)
            for k in range(2):
                for tt in range(TT):
                    pool.indirect_dma_start(out=slot_d, out_offset=bass.IndirectOffsetOnAxis(ap=sli[:, k, tt:tt + 1], axis=0),
                                            in_=toki[:, tt:tt + 1], in_offset=None).then_inc(sem("idx_stored"), 16)
            pool.wait_ge(sem("idx_stored"), 128)
            pool.wait_ge(sem("xn_stored"), 16)
            for me in ("pe", "act", "dve"):
                pool.wait_ge(phase[me], PH_MOE)
            blocks = pool.value_load(nbi[0:1, 0:1], min_val=1, max_val=NBLK)
            slot_rows = slot_d.rearrange("(b s) o -> b s o", s=BLK)
            def gather(block, w, before):
                pool.wait_ge(sem(f"t_done{w}"), before + 1)
                pool.dma_start(IDX[w][:, :], slot_rows[block]).then_inc(sem(f"id_landed{w}"), 16)
                pool.wait_ge(sem(f"id_landed{w}"), before * 16 + 16)
                pool.sem_inc(sem("pool_passed"), 1)
                pool.indirect_dma_start(out=xg[w], out_offset=None, in_=xn2_d,
                                        in_offset=bass.IndirectOffsetOnAxis(ap=IDX[w][:, 0:1], axis=0)).then_inc(sem(f"xg_landed{w}"), 16)

            gather(0, 0, 0)
            with pool.Fori(0, NBLK // 2) as i:
                with pool.If(i * 2 < blocks):
                    gather(i * 2 + 1, 1, i)
                    gather(i * 2 + 2, 0, i + 1)
            for me in ("act", "dve", "pe"):
                pool.wait_ge(phase[me], PH_MOE + 1)
            for tt in range(TT):
                if tt >= 2:
                    pool.wait_ge(sem("picked_used"), tt - 1)
                for k in range(2):
                    pool.indirect_dma_start(out=picked[tt % 2][k], out_offset=None, in_=ys_d,
                                            in_offset=bass.IndirectOffsetOnAxis(ap=sli[:, k, tt:tt + 1], axis=0)).then_inc(sem(f"picked_landed{tt % 2}"), 16)

        @block.tensor
        def _(pe):
            def claim(key):
                b, n = use[key]
                if n:
                    pe.wait_ge(bank_free[b], n)
                return ps[b]

            def full(ins, key):
                ins.then_inc(bank_full[use[key][0]], 1)
                last[0] = (bank_full[use[key][0]], use[key][1] + 1)

            last = [None]

            def bar():
                pe.wait_ge(*last[0])
                barrier(pe, "pe")

            def transposes(key, srcs):
                bk = claim(key)
                for n, src in enumerate(srcs):
                    ins = nc.tensor.transpose(bk[0:src.shape[1], n * P:n * P + src.shape[0]], src, ident[0:src.shape[0], 0:src.shape[0]])
                full(ins, key)

            def project(c):
                kind, w, col, width, kk, token_major = chunks[c]
                act = {"out": M, "out2": yT}.get(kind, X)
                banks = []
                for kt in range(kk):
                    s, count = load_of[c, kt // 4]
                    if kt % 4 == 0:
                        pe.wait_ge(w_landed[s], count)
                    for j in range(4):
                        key = ("P", c, j)
                        if kt == 0:
                            banks.append(claim(key))
                        if token_major:
                            ins = nc.tensor.matmul(banks[j][:, 0:width], act[:, kt, j * P:(j + 1) * P], W[:, s, kt % 4, 0:width],
                                                   start=kt == 0, stop=kt == kk - 1)
                        else:
                            ins = nc.tensor.matmul(banks[j][:, :], W[:, s, kt % 4, j * P:(j + 1) * P], act[:, kt, :],
                                                   start=kt == 0, stop=kt == kk - 1)
                        if kt == kk - 1:
                            full(ins, key)
                            if j == 3:
                                pe.wait_ge(*last[0])
                                pe.sem_inc(slot_free, 1)
                        elif kt % 4 == 3 and j == 3:
                            ins.then_inc(slot_free, 1)

            def mod_sum(v):
                bk = claim(("mod", v))
                pe.wait_ge(mod_ready, v + 1)
                for kt in range(KD):
                    ins = nc.tensor.matmul(bk[:, kt:kt + 1], macc[:, kt:D:KD], C["ones"][:, 0:1], start=True, stop=True)
                full(ins, ("mod", v))

            def post(c):
                kind = chunks[c][0]
                i = c - first[kind]
                for key in posts(c):
                    j = key[2]
                    if kind == "xbc":
                        pe.wait_ge(sem("silu_done"), 4 * i + j + 1)
                        src = SL[:, j, :] if i < 2 else bfm[:, j, :]
                        transposes(key, [src[:, tt * P:(tt + 1) * P] for tt in range(TT)])
                    elif kind == "small":
                        pe.wait_ge(sem("ki_ready"), 1)
                        transposes(key, [TK[:, tt, :] for tt in range(TT)])
                    elif kind in ("q2", "k2"):
                        pe.wait_ge(sem("norm_ready"), 2 if kind == "k2" else 1)
                        transposes(key, [T2[:, tt, j * P:(j + 1) * P] for tt in range(TT)])
                    else:
                        pe.wait_ge(sem("rope_ready"), c - first["qi"] + 1)
                        transposes(key, [T[:, tt, j * P:(j + 1) * P] for tt in range(TT)])

            def index_scores():
                pe.wait_ge(sem("index_turned"), 1)
                for hd, i in IX:
                    bk = claim(("IX", i, hd))
                    lo, nk = 64 * (hd % 2), (i + 1) * P
                    full(nc.tensor.matmul(bk[:, 0:nk], qiT[lo:lo + 64, hd // 2, i * P:nk], kiT[lo:lo + 64, 0:nk], start=True, stop=True),
                         ("IX", i, hd))

            def step_sums():
                bk = claim("cum")
                pe.wait_ge(sem("dtA_ready"), 1)
                flat = dtA[:, :, :].rearrange("p t h -> p (t h)")
                nc.tensor.matmul(bk[:, 0:64], C["upto"], flat, start=True, stop=True)
                full(nc.tensor.matmul(bk[:, 64:128], C["ones"], flat, start=True, stop=True), "cum")

            def stage(n):
                for c in STAGES[n]:
                    project(c)
                    if c in MODSUM:
                        mod_sum(MODSUM[c])
                    if c > STAGES[n][0]:
                        post(c - 1)
                    if c == CUM_AT:
                        step_sums()
                    if c == IX_AT:
                        index_scores()
                post(STAGES[n][-1])

            pe.wait_ge(sem("const_landed"), 16)
            for tt in range(TT):
                pe.wait_ge(x_landed, 16 * TT)
            for kt in range(KD):
                transposes(("xT", kt), [Hx[:, tt, kt, :] for tt in range(TT)])
            pe.wait_ge(small_landed, 16 * N_SMALL)
            transposes("pack", [packrow[0:102, :]])
            pe.wait_ge(xT_dve, 8)
            pe.wait_ge(xT_act, 8)
            stage(0)
            bar()

            def ssd_front(i):
                c, g = divmod(i, SG)
                bk = claim(("G", i))
                full(nc.tensor.matmul(bk[:, 0:P], bfm[:, g, c * P:(c + 1) * P], cfm[:, g, c * P:(c + 1) * P], start=True, stop=True), ("G", i))
                bk = claim(("AC", i))
                nc.tensor.matmul(bk[:, :], C["before"], neg_ident.unsqueeze(1).to_broadcast([P, SR, P]), start=True, stop=True)
                for r in range(SR):
                    ins = nc.tensor.matmul(bk[:, r * P:(r + 1) * P], dtA[:, c, 4 * g + r:4 * g + r + 1].to_broadcast([P, P]), C["upto"],
                                           start=False, stop=True, skip_group_check=True)
                full(ins, ("AC", i))

            def ssd_back(i):
                c, g = divmod(i, SG)
                bk = claim(("Y", i))
                pe.wait_ge(sem("decay_ready"), i + 1)
                pe.wait_ge(sem("xd_ready"), c + 1)
                for r in range(SR):
                    h = 4 * g + r
                    ins = nc.tensor.matmul(bk[:, r * 64:(r + 1) * 64], Mt[:, i % 2, r, :], xdt[:, c % 2, h * 64:(h + 1) * 64], start=True, stop=True)
                if c:
                    pe.wait_ge(sem("state_ready"), i - 3)
                    ins = nc.tensor.matmul(bk[:, 256:512], cfm[:, g, c * P:(c + 1) * P], Hst[:, g * 256:(g + 1) * 256], start=True, stop=True)
                full(ins, ("Y", i))
                if i < 12:
                    bk = claim(("ST", i))
                    full(nc.tensor.matmul(bk[:, 0:256], btm[:, c, g * P:(g + 1) * P], xdd[:, c % 2, g * 256:(g + 1) * 256], start=True, stop=True), ("ST", i))

            ssd_front(0)
            for i in range(16):
                if i < 15:
                    ssd_front(i + 1)
                ssd_back(i)
            for ct in range(8):
                pe.wait_ge(sem("gated_ready"), 16)
                transposes(("ZT", ct), [Z[:, tt, ct * P:(ct + 1) * P] for tt in range(TT)])
            bar()
            stage(1)
            bar()

            def logits(k):
                i, g = GROUPS[k]
                for r in range(4):
                    key = ("S", i, 4 * g + r)
                    bk = claim(key)
                    nk = (i + 1) * P
                    full(nc.tensor.matmul(bk[:, 0:nk], qT[:, 4 * g + r, i * P:nk], kT[:, g, 0:nk], start=True, stop=True), key)

            logits(0)
            turned = 0
            for k, (i, g) in enumerate(GROUPS):
                if k + 1 < len(GROUPS):
                    logits(k + 1)
                pe.wait_ge(sem("probs_ready"), k + 1)
                for kb in range(i + 1):
                    transposes(("PT", i, g, kb), [Pb[k % 2][:, r, kb * P:(kb + 1) * P] for r in range(4)])
                bk = claim(("PV", i, g))
                for kb in range(i + 1):
                    turned += 1
                    pe.wait_ge(sem("pt_ready"), turned)
                    ins = nc.tensor.matmul(bk[:, :], V[:, kb, g * P:(g + 1) * P], PT[k % 2][:, kb, :], start=kb == 0, stop=kb == i)
                full(ins, ("PV", i, g))
            bar()
            stage(2)
            bar()
            pe.wait_ge(sem("xn_ready"), 2)
            pe.wait_ge(sem("xn_ready_act"), 2)
            for kt in range(KD):
                transposes(("hT", kt), [XNx[:, tt, kt, :] for tt in range(TT)])
            pe.wait_ge(sem("late_landed"), 64)
            transposes("wsT", [WS[:, g, :] for g in range(4)])
            bar()
            stage(3)
            bar()

            for tt in range(TT):
                bk = claim(("SPG", tt))
                for g in range(4):
                    ins = nc.tensor.matmul(bk[:, g * P:(g + 1) * P], WS[:, g, :], VA[:, tt, g * P:(g + 1) * P], start=True, stop=True)
                full(ins, ("SPG", tt))
            def scores(h):
                for j in range(4):
                    bk = claim(("Z", h, j))
                    n = S - P * j
                    full(nc.tensor.matmul(bk[:, 0:n], kT2[:, h, j * P:(j + 1) * P], qT2[:, h, j * P:S], start=True, stop=True), ("Z", h, j))

            def log_a(h):
                pe.wait_ge(sem("fail_ready"), h + 1)
                for j in range(4):
                    bk = ps[use["Z", h, j][0]]
                    n = S - P * j
                    for jj in range(j, 4):
                        nc.tensor.matmul(bk[:, (jj - j) * P:n], C["neg_from"] if jj == j else C["neg_ones"], tri(SPall[h % 2], jj),
                                         start=False, stop=False, skip_group_check=True)
                    ins = nc.tensor.matmul(bk[:, 0:P], ident, C["not_before"], start=False, stop=True, skip_group_check=True)
                    ins.then_inc(sem("log_a_ready"), 1)

            def values(h):
                pe.wait_ge(sem("a_ready"), h + 1)
                bk = claim(("O", h))
                for i in range(TT):
                    for j in range(i + 1):
                        ins = nc.tensor.matmul(bk[:, i * P:(i + 1) * P], tri(ATall[h % 2], j)[:, (i - j) * P:(i - j + 1) * P], V2[:, j, h * P:(h + 1) * P],
                                               start=j == 0, stop=j == i)
                full(ins, ("O", h))

            scores(0)
            scores(1)
            for h in (0, 2):
                log_a(h)
                log_a(h + 1)
                values(h)
                if h == 0:
                    scores(2)
                values(h + 1)
                if h == 0:
                    scores(3)
            pe.wait_ge(sem("y_ready"), 1)
            for ct in range(8):
                transposes(("yT", ct), [Y[:, tt, ct * P:(ct + 1) * P] for tt in range(TT)])
            bar()
            stage(4)
            bar()
            pe.wait_ge(sem("xn_ready"), 4)
            pe.wait_ge(sem("xn_ready_act"), 4)
            for kt in range(KD):
                transposes(("h2T", kt), [XNx[:, tt, kt, :] for tt in range(TT)])
            pe.wait_ge(sem("h2T_dve"), 8)
            pe.wait_ge(sem("h2T_act"), 8)
            bk = claim("router")
            for tt in range(TT):
                for kt in range(KD):
                    ins = nc.tensor.matmul(bk[:, tt * 36:(tt + 1) * 36], X[:, kt, tt * P:(tt + 1) * P], WR[:, kt, :], start=kt == 0, stop=kt == KD - 1)
            full(ins, "router")
            pe.wait_ge(sem("choice_ready"), 1)
            bk = claim("rank")
            for tt in range(TT):
                for s in range(tt + 1):
                    nc.tensor.matmul(bk[:, tt * NE:(tt + 1) * NE], C["before"] if s == tt else C["ones"], EM[:, s, :], start=s == 0, stop=s == tt)
            for s in range(TT):
                ins = nc.tensor.matmul(bk[:, P:P + NE], C["ones"], EM[:, s, :], start=s == 0, stop=s == TT - 1)
            full(ins, "rank")
            bar()

            pe.wait_ge(sem("routed"), 1)
            blocks = pe.value_load(nbi[0:1, 0:1], min_val=1, max_val=NBLK)
            for name in ("up_done", "down_done", "t_done"):
                for u in range(2):
                    pe.sem_inc(sem(f"{name}{u}"), 1)

            def turn(block, w, before):
                pe.wait_ge(sem(f"xg_landed{w}"), before * 16 + 16)
                if block is not None:
                    pe.wait_ge(sem("t_taken"), block + 1)
                pe.sem_inc(sem("pe_passed"), 1)
                for kt in range(KD):
                    ins = nc.tensor.transpose(ps[kt // 8][:, (kt % 8) * BLK:(kt % 8 + 1) * BLK], xgx[w][:, kt, :], ident[0:BLK, 0:BLK])
                ins.then_inc(sem(f"t_done{w}"), 1)

            turn(None, 0, 0)
            with pe.Fori(0, NBLK // 2) as i:
                with pe.If(i * 2 < blocks):
                    for u in range(2):
                        pe.wait_ge(sem("xt_ready"), i * 2 + u + 1)
                        pe.wait_ge(sem("h_ready"), i * 2 + u + 1)
                        for w, bk, land in ((WGt[u], ps[2], f"wg_landed{u}"), (WUt[u], ps[3], f"wu_landed{u}")):
                            pe.wait_ge(sem(land), i * 16 + 16)
                            for m in range(2):
                                for kt in range(KD):
                                    ins = nc.tensor.matmul(bk[:, m * BLK:(m + 1) * BLK], w[:, kt, m * P:(m + 1) * P], xgT[u][:, kt, :],
                                                           start=kt == 0, stop=kt == KD - 1)
                        ins.then_inc(sem(f"up_done{u}"), 1)
                        turn(i * 2 + u + 1, 1 - u, i + u)
                        pe.wait_ge(sem("h_ready"), i * 2 + u + 2)
                        pe.wait_ge(sem(f"wd_landed{u}"), i * 16 + 16)
                        pe.wait_ge(sem("y_taken_dve"), i * 2 + u + 1)
                        for n in range(4):
                            for m in range(2):
                                ins = nc.tensor.matmul(ps[4 + n][0:BLK, :], hb[u][:, m, :], WDt[u][:, m, n * 512:(n + 1) * 512], start=m == 0, stop=m == 1)
                        ins.then_inc(sem(f"down_done{u}"), 1)
            pe.sem_inc(phase["pe"], 1)

        @block.scalar
        def _(act):
            st = Steps(act, sem("act_done"))

            def fn(dst, src, func, s=None, v=None, **kw):
                st.do(nc.scalar.activation(dst, src, func, **kw), s, v)

            def bar():
                st.settle()
                barrier(act, "act")

            for tt in range(TT):
                act.dma_start(H[:, tt, :], a["x"][0, tt * P:(tt + 1) * P, :]).then_inc(x_landed, 16)
            act.wait_ge(small_landed, 16 * N_SMALL)
            fn(csil[:, :], ccol[:, :], ACT.Silu, sem("csil_ready"))
            for kt in range(1, KD, 2):
                bk = filled(act, ("xT", kt))
                fn(X[:, kt, :], bk[:, :], ACT.Copy, *freed(("xT", kt)))
            st.settle()
            act.sem_inc(xT_act, 8)

            def take_post(c):
                kind = chunks[c][0]
                i = c - first[kind]
                for key in posts(c):
                    j = key[2]
                    bk = filled(act, key)
                    if kind == "xbc":
                        src = bk[:, :].rearrange("p (t e) -> p t e", t=TT)
                        dst = xs[:, :, (4 * i + j) * P:(4 * i + j + 1) * P] if i < 2 else btm[:, :, j * P:(j + 1) * P]
                        fn(dst, src, ACT.Copy, *freed(key))
                    elif kind == "small":
                        fn(kiT, bk[:, :], ACT.Copy, *freed(key))
                    elif kind == "q":
                        fn(qT[:, 4 * i + j, :], bk[:, :], ACT.Copy, *freed(key))
                    elif kind == "kv":
                        fn(kT[:, j, :], bk[:, :], ACT.Copy, *freed(key))
                    elif kind == "qi":
                        fn(qiT[:, 4 * i + j, :], bk[:, :], ACT.Copy, *freed(key))
                    elif kind == "q2":
                        fn(qT2[:, j, :], bk[:, :], ACT.Copy, *freed(key), scale=pack[:, 102:103])
                    elif kind == "k2":
                        fn(kT2[:, j, :], bk[:, :], ACT.Copy, *freed(key), scale=pack[:, 97:98])

            def work(c):
                kind = chunks[c][0]
                i = c - first[kind]
                for j in range(4):
                    key = ("P", c, j)
                    if kind == "xbc":
                        act.wait_ge(sem("conv_done"), 4 * i + j + 1)
                        dst = SL[:, j, :] if i < 2 else (bfm if i == 2 else cfm)[:, j, :]
                        fn(dst, CV[:, j % 2, :], ACT.Silu, sem("silu_done"))
                    elif kind == "z":
                        if i == 0 and j == 0:
                            act.wait_ge(sem("idx_cleared"), 16)
                        fn(Z[:, j, i * 512:(i + 1) * 512], filled(act, key)[:, :], ACT.Silu, *freed(key))
                    elif kind == "small":
                        fn(SM[:, j, :], filled(act, key)[:, 0:96], ACT.Copy, *freed(key))
                    elif kind in ("q", "kv", "qi"):
                        bk = filled(act, key)
                        if kind == "kv":
                            fn(V[:, j, :], bk[:, 256:512], ACT.Copy)
                        fn(T[:, j, :], bk[:, :], ACT.Copy, *freed(key))
                    elif kind == "za":
                        fn(M[:, 4 * i + j, :], filled(act, key)[:, :], ACT.Silu, *freed(key))
                    elif kind in ("va", "ua"):
                        fn((VA if kind == "va" else UA)[:, j, :], filled(act, key)[:, :], ACT.Gelu, *freed(key))
                    elif kind in ("q2", "k2"):
                        bk = filled(act, key)
                        fn(T2[:, j, :], bk[:, :], ACT.Copy)
                        fn(SQ[:, j, :], bk[:, :], ACT.Square, *freed(key))
                    elif kind == "out2":
                        act.wait_ge(sem("part_ready"), 4 * i + j + 1)
                        fn(junk[:, 0:512], H[:, j, i * 512:(i + 1) * 512], ACT.Square, accum_out=ss[:, 4 * j + i:4 * j + i + 1])
                        st.settle()
                        act.sem_inc(sem("part_squared"), 1)
                    elif kind == "v2":
                        fn(V2[:, j, :], filled(act, key)[:, :], ACT.Copy, *freed(key))
                if kind in ("small", "q", "kv", "qi", "va", "q2", "k2"):
                    st.settle()
                    act.sem_inc(sem("copied"), 1)
                if kind in ("va", "q2", "k2"):
                    act.wait_ge(sem("mean_ready"), ("va", "q2", "k2").index(kind) + 1)
                    fn(rs[:, 0:16], rs[:, 0:16], ACT.Sqrt, sem("root_ready"))

            def stage(n):
                for c in STAGES[n]:
                    if c > STAGES[n][0]:
                        take_post(c - 1)
                    if c == IX_AT:
                        st.settle()
                        act.sem_inc(sem("index_turned"), 1)
                    if c == CUM_AT:
                        act.wait_ge(sem("cum_ready"), 1)
                        fn(eac[:, :, :], nacum[:, :, :], ACT.Exp, scale=-1.0)
                        fn(cdec[:, :, :], tot[:, :, :], ACT.Exp)
                        fn(dec[:, :, :], dec[:, :, :], ACT.Exp, sem("cum_exp"))
                    work(c)
                    if chunks[c][0] == "small":
                        act.wait_ge(sem("dt_in"), 1)
                        fn(dna[:, :, :], dna[:, :, :], ACT.Exp)
                        fn(ea[:, :], alog[:, :], ACT.Exp)
                        st.settle()
                        fn(dna[:, :, :], dna[:, :, :], ACT.Ln, sem("dt_log"), bias=1.0)
                    if c == IX_AT:
                        for n_relu, (hd, i) in enumerate(IX):
                            bk = filled(act, ("IX", i, hd))
                            if n_relu >= len(R):
                                act.wait_ge(sem("relu_used"), n_relu - len(R) + 1)
                            nk = (i + 1) * P
                            fn(R[n_relu % len(R)][:, 0:nk], bk[:, 0:nk], ACT.Relu, *freed(("IX", i, hd)))
                take_post(STAGES[n][-1])

            stage(0)
            bar()
            def decays(i):
                c, g = divmod(i, SG)
                bk = filled(act, ("AC", i))
                if i >= 2:
                    act.wait_ge(sem("decay_ready"), i - 1)
                for r in range(SR):
                    h = 4 * g + r
                    fn(Dm[:, i % 2, r, :], bk[:, r * P:(r + 1) * P], ACT.Exp, *(freed(("AC", i)) if r == SR - 1 else (None, None)),
                       bias=nacum[:, c, h:h + 1])
                st.settle()
                act.sem_inc(sem("diff_exp"), 1)

            def squares(i):
                c, g = divmod(i, SG)
                act.wait_ge(sem("gate_done"), i + 1)
                fn(sqj, Z[:, c, g * 256:(g + 1) * 256], ACT.Square, accum_out=ss[:, i:i + 1])
                st.settle()
                act.sem_inc(sem("ms_summed"), 1)

            for i in range(16):
                decays(i)
                if i >= 2:
                    squares(i - 2)
            squares(14)
            squares(15)
            act.wait_ge(sem("ms_ready"), 1)
            fn(rs[:, 0:16], rs[:, 0:16], ACT.Sqrt, sem("ms_root"))
            for ct in range(8):
                fn(M[:, 8 + ct, :], filled(act, ("ZT", ct))[:, :], ACT.Copy, *freed(("ZT", ct)), scale=pack[:, 80 + ct:81 + ct])
            bar()
            stage(1)
            bar()
            def exps(k):
                i, g = GROUPS[k]
                nk = (i + 1) * P
                act.wait_ge(sem("max_ready"), k + 1)
                for r in range(4):
                    p = Pb[k % 2][:, r, 0:nk]
                    fn(p, p, ACT.Exp, bias=nm[:, k % 2, r:r + 1], accum_out=sm[:, k % 2, r:r + 1])
                st.settle()
                act.sem_inc(sem("exp_done"), 1)

            exps(0)
            for k, (i, g) in enumerate(GROUPS):
                if k + 1 < len(GROUPS):
                    exps(k + 1)
                if k >= 2:
                    filled(act, ("PV", *GROUPS[k - 2]))
                for kb in range(i + 1):
                    key = ("PT", i, g, kb)
                    fn(PT[k % 2][:, kb, :], filled(act, key)[:, :], ACT.Copy, *freed(key))
                    st.settle()
                    act.sem_inc(sem("pt_ready"), 1)
            bar()
            for tt in range(TT):
                act.dma_start(H[:, tt, :], a["x"][0, tt * P:(tt + 1) * P, :]).then_inc(x_landed, 16)
            act.dma_start(lng, bcast_row(a["ln_g"][0])).then_inc(sem("ln_landed"), 16)
            act.dma_start(lnb, bcast_row(a["ln_b"][0])).then_inc(sem("ln_landed"), 16)
            bar()
            act.dma_start(gmg, bcast_row(a["gm_norm_g_2"][0])).then_inc(sem("late_landed"), 16)
            act.dma_start(WS, a["gm_ws_2"][0].rearrange("g t q -> t g q")).then_inc(sem("late_landed"), 16)
            act.dma_start(WR[:, :, 0:4], a["w_group_2"][0].rearrange("(p k) n -> p k n", k=KD)).then_inc(sem("late_landed"), 16)
            act.dma_start(WR[:, :, 4:36], a["w_route_2"][0].rearrange("(p k) n -> p k n", k=KD)).then_inc(sem("late_landed"), 16)
            act.wait_ge(sem("var_ready"), 1)
            act.wait_ge(sem("ys_cleared"), 16)
            fn(rs[:, 0:4], rs[:, 0:4], ACT.Sqrt, sem("var_root"))

            def norm_hidden(n):
                act.wait_ge(sem("msq_ready"), n + 1)
                fn(rs[:, 0:4], rs[:, 0:4], ACT.Sqrt, sem("msq_root"))
                st.settle()
                for tt in range(TT // 2, TT):
                    fn(XN[:, tt, :], H[:, tt, :], ACT.Copy, sem("xn_ready_act"), scale=rs[:, tt:tt + 1])

            act.wait_ge(sem("shift_ready"), 1)
            for tt in range(TT):
                fn(H[:, tt, :], H[:, tt, :], ACT.Identity, sem("standard_row"), scale=rs[:, tt:tt + 1], bias=mv[:, tt, 0:1])
            for tt in range(TT):
                act.wait_ge(sem("h_rows"), tt + 1)
                fn(junk, H[:, tt, :], ACT.Square, accum_out=ss[:, tt:tt + 1])
                st.settle()
            act.sem_inc(sem("squares_done"), 1)
            norm_hidden(0)
            for kt in range(1, KD, 2):
                key = ("hT", kt)
                fn(X[:, kt, :], filled(act, key)[:, :], ACT.Identity, *freed(key), scale=G1[:, kt:kt + 1], bias=MV[:, 0, kt:kt + 1])
            bar()
            stage(3)
            bar()
            def soften(h):
                act.wait_ge(sem("abs_ready"), h + 1)
                fn(EAall[h % 2], EAall[h % 2], ACT.Exp)
                st.settle()

            for pair in (0, 2):
                for h in (pair, pair + 1):
                    soften(h)
                for h in (pair, pair + 1):
                    fn(EAall[h % 2], EAall[h % 2], ACT.Ln, sem("log_ready"), bias=1.0)
                for h in (pair, pair + 1):
                    if h >= 2:
                        filled(act, ("O", h - 2))
                    for j in range(4):
                        act.wait_ge(sem("log_a_ready"), 4 * h + j + 1)
                        fn(tri(ATall[h % 2], j), ps[use["Z", h, j][0]][:, 0:S - P * j], ACT.Exp, *freed(("Z", h, j)))
                    st.settle()
                    act.sem_inc(sem("a_ready"), 1)
            act.wait_ge(sem("mean_ready"), 4)
            fn(rs[:, 0:32], rs[:, 0:32], ACT.Sqrt, sem("root_ready"))
            for ct in range(8):
                key = ("yT", ct)
                fn(yT[:, ct, :], filled(act, key)[:, :], ACT.Copy, *freed(key), scale=pack[:, 88 + ct:89 + ct])
            bar()
            act.wait_ge(sem("mod_out"), 6)
            for n, v in enumerate((2, 5)):
                act.dma_start(gates_d[n].rearrange("(p k) -> p k", k=KD), MV[:, v, :]).then_inc(sem("gate_stored"), 16)
            act.wait_ge(sem("gate_stored"), 32)
            act.dma_start(gate, bcast_row(gates_d[0])).then_inc(sem("gate_landed"), 16)
            act.dma_start(gate2, bcast_row(gates_d[1])).then_inc(sem("gate_landed"), 16)
            stage(4)
            bar()
            norm_hidden(1)
            for kt in range(1, KD, 2):
                key = ("h2T", kt)
                fn(X[:, kt, :], filled(act, key)[:, :], ACT.Identity, *freed(key), scale=G2[:, kt:kt + 1], bias=MV[:, 3, kt:kt + 1])
            st.settle()
            act.sem_inc(sem("h2T_act"), 8)
            act.dma_start(xn2_d.rearrange("(t p) d -> p t d", p=P), XN).then_inc(sem("xn_stored"), 16)
            act.wait_ge(sem("group_in"), 1)
            fn(r4[:, :, :], r4[:, :, :], ACT.Exp, sem("group_exp"))
            act.wait_ge(sem("pair_in"), 1)
            fn(e2v[:, :], e2v[:, :], ACT.Exp, sem("pair_exp"))
            act.wait_ge(sem("xn_stored"), 16)
            bar()
            act.wait_ge(sem("routed"), 1)
            blocks = act.value_load(nbi[0:1, 0:1], min_val=1, max_val=NBLK)
            ysb = ys_d.rearrange("(b s) d -> b s d", s=BLK)
            for u in range(2):
                act.sem_inc(sem(f"y_stored{u}"), 16)
            with act.Fori(0, NBLK // 2) as i:
                with act.If(i * 2 < blocks):
                    for u in range(2):
                        act.wait_ge(sem(f"up_done{u}"), i + 2)
                        nc.scalar.activation(SGt[u], ps[2][:, 0:P], ACT.Silu).then_inc(sem("silu_gate"), 1)
                        act.wait_ge(sem("y_taken_dve"), i * 2 + u + 2)
                        act.dma_start(ysb[i * 2 + u], yb[u]).then_inc(sem(f"y_stored{u}"), 16)
            pairs = (blocks + 1) // 2
            act.wait_ge(sem("y_stored0"), pairs * 16 + 16)
            act.wait_ge(sem("y_stored1"), pairs * 16 + 16)
            act.sem_inc(phase["act"], 1)
            for me in ("dve", "pe"):
                act.wait_ge(phase[me], PH_MOE + 1)
            for tt in range(TT):
                act.wait_ge(sem("out_ready"), tt + 1)
                act.dma_start(out[0, tt * P:(tt + 1) * P, :], H[:, tt, :]).then_inc(sem("out_stored"), 16)
            act.wait_ge(sem("out_stored"), 16 * TT)

        @block.vector
        def _(dve):
            v = nc.vector
            st = Steps(dve, sem("dve_done"))

            def bar():
                st.settle()
                barrier(dve, "dve")

            def tt_(dst, x, y, op, s=None, n=None):
                st.do(v.tensor_tensor(dst, x, y, op), s, n)

            def ts(dst, x, s1, s2, op0, op1=None, s=None, n=None):
                if op1 is None:
                    st.do(v.tensor_scalar(dst, x, s1, None, op0), s, n)
                else:
                    st.do(v.tensor_scalar(dst, x, s1, s2, op0, op1), s, n)

            def stt(dst, x, sc, y, op0, op1, s=None, n=None):
                st.do(v.scalar_tensor_tensor(out=dst, in0=x, scalar=sc, in1=y, op0=op0, op1=op1), s, n)

            def per(x, shape):
                return x.unsqueeze(len(x.shape)).to_broadcast(shape)

            mod_step = [0]

            def mod_steps(n):
                for _ in range(n):
                    s = mod_step[0]
                    vec, kt = divmod(s, KD)
                    dve.wait_ge(mod_landed[s % 2], 16 * (s // 2 + 1))
                    if kt == 0:
                        if s:
                            filled(dve, ("mod", vec - 1))
                        ts(macc, mring[:, s % 2, :], csil[:, kt:kt + 1], None, ALU.mult, s=mod_used)
                    else:
                        st.settle()
                        stt(macc, mring[:, s % 2, :], csil[:, kt:kt + 1], macc, ALU.mult, ALU.add, s=mod_used)
                    mod_step[0] += 1
                    if kt == KD - 1:
                        st.settle()
                        dve.sem_inc(mod_ready, 1)

            def mod_take(vec):
                key = ("mod", vec)
                bk = filled(dve, key)
                tt_(MV[:, vec, :], bk[:, 0:KD], bmod[:, vec, :], ALU.add, *freed(key))
                st.settle()
                tt_(MV[:, vec, :], MV[:, vec, :], lmod[:, vec, :], ALU.add, sem("mod_out"))
                st.settle()

            def time_steps():
                ts(neg_ident, ident, NEG, None, ALU.mult)
                tt_(dtx[:, :, :], SM[:, :, 80:96], dtb[:, :].unsqueeze(1).to_broadcast([P, TT, 16]), ALU.add)
                st.settle()
                ts(dmx[:, :, :], dtx[:, :, :], 0.0, None, ALU.max)
                stt(dna[:, :, :], dtx[:, :, :], -1.0, dtx[:, :, :], ALU.mult, ALU.min, s=sem("dt_in"))
                dve.wait_ge(sem("dt_log"), 1)
                tt_(dt_[:, :, :], dna[:, :, :], dmx[:, :, :], ALU.add)
                st.settle()
                stt(dtA[:, :, :], dt_[:, :, :], -1.0, ea[:, :].unsqueeze(1).to_broadcast([P, TT, 16]), ALU.mult, ALU.mult, s=sem("dtA_ready"))

            def take_sums():
                bk = filled(dve, "cum")
                ts(nacum[:, :, :].rearrange("p t h -> p (t h)"), bk[:, 0:64], -1.0, None, ALU.mult)
                st.do(v.tensor_copy(tot[:, :, :].rearrange("p t h -> p (t h)"), bk[:, 64:128]), *freed("cum"))
                st.settle()
                tt_(dec[:, :, :], tot[:, :, :], nacum[:, :, :], ALU.add, s=sem("cum_ready"))

            def index_sums():
                for m, (hd, i) in enumerate(IX):
                    nk = (i + 1) * P
                    sem_, n = freed(("IX", i, hd))
                    filled(dve, ("IX", i, hd))
                    dve.wait_ge(sem_, n)
                    w = wi[:, i, hd:hd + 1]
                    r = R[m % len(R)][:, 0:nk]
                    if hd == 0:
                        ts(BIAS[i], r, w, None, ALU.mult, s=sem("relu_used"))
                    else:
                        dve.wait_ge(sem("relu_used"), m + 1 - (TT - 1))
                        stt(BIAS[i], r, w, BIAS[i], ALU.mult, ALU.add, s=sem("relu_used"))

            def choose():
                ts(BIAS[0], C["late_chunk"], NEG, None, ALU.mult)
                done = [0] * TT

                def step(i, ins):
                    st.do(ins)
                    done[i] = st.n

                dve.wait_ge(sem("relu_used"), len(IX))
                for i in range(1, TT):
                    diag = BIAS[i][:, i * P:(i + 1) * P]
                    step(i, v.scalar_tensor_tensor(out=diag, in0=C["late_chunk"], scalar=OUT_OF_REACH, in1=diag, op0=ALU.mult, op1=ALU.add))
                for _ in range(TOPK // 8):
                    for i in range(1, TT):
                        dve.wait_ge(st.own, done[i])
                        step(i, v.max(m8[:, i, :], BIAS[i]))
                    for i in range(1, TT):
                        dve.wait_ge(st.own, done[i])
                        step(i, v.match_replace(out=BIAS[i], in_to_replace=m8[:, i, :], in_values=BIAS[i], imm_value=TAKEN))
                for i in range(1, TT):
                    dve.wait_ge(st.own, done[i])
                    step(i, v.tensor_scalar(BIAS[i], BIAS[i], -3.35e38, NEG, ALU.is_gt, ALU.mult))

            def mod_hook(c):
                if c < 18:
                    mod_steps((6, 5, 5)[c % 3])

            dve.wait_ge(sem("const_landed"), 16)
            dve.wait_ge(small_landed, 16 * N_SMALL)
            for kt in range(0, KD, 2):
                st.do(v.tensor_copy(X[:, kt, :], filled(dve, ("xT", kt))[:, :]), *freed(("xT", kt)))
            st.settle()
            dve.sem_inc(xT_dve, 8)
            st.do(v.tensor_copy(pack[:, 0:102], filled(dve, "pack")[:, 0:102]), *freed("pack"))
            st.settle()
            ts(pack[:, 102:103], pack[:, 96:97], float(DH) ** -0.5, None, ALU.mult)
            dve.wait_ge(sem("csil_ready"), 1)

            def rotate(view, cos, sin, heads, half):
                for tt in range(TT):
                    x = view[:, tt]
                    n = heads * 2 * half
                    A = RT[:, 0, 0:n].rearrange("p (h d) -> p h d", h=heads)
                    B = RT[:, 1, 0:n].rearrange("p (h d) -> p h d", h=heads)
                    co = C[cos][:, tt * 2 * half:(tt + 1) * 2 * half].unsqueeze(1).to_broadcast([P, heads, 2 * half])
                    si = C[sin][:, tt * 2 * half:(tt + 1) * 2 * half].unsqueeze(1).to_broadcast([P, heads, 2 * half])
                    tt_(A, x, co, ALU.mult)
                    tt_(B, x, si, ALU.mult)
                    st.settle()
                    tt_(x[:, :, 0:half], A[:, :, 0:half], B[:, :, half:2 * half], ALU.add)
                    tt_(x[:, :, half:2 * half], A[:, :, half:2 * half], B[:, :, 0:half], ALU.add)
                    st.settle()

            def inv_mean(dst, src, n, eps, s):
                ts(dst, src, 1.0 / n, eps, ALU.mult, ALU.add)
                st.settle()
                st.do(v.reciprocal(dst, dst), s)

            def work(c):
                kind = chunks[c][0]
                i = c - first[kind]
                if kind == "xbc":
                    for j in range(4):
                        key = ("P", c, j)
                        bk = filled(dve, key)
                        e = 4 * i + j
                        if e >= 2:
                            dve.wait_ge(sem("silu_done"), e - 1)
                        y = CV[:, j % 2, :]
                        ts(y, bk[:, :], pack[:, 48 + e:49 + e], pack[:, 64 + e:65 + e], ALU.mult, ALU.add)
                        for k in (1, 2, 3):
                            st.settle()
                            stt(y[:, k:S], bk[:, 0:S - k], pack[:, 16 * (3 - k) + e:16 * (3 - k) + e + 1], y[:, k:S], ALU.mult, ALU.add,
                                *(freed(key) if k == 3 else (None, None)))
                        st.settle()
                        dve.sem_inc(sem("conv_done"), 1)
                elif kind == "small":
                    dve.wait_ge(sem("copied"), 1)
                    for half in range(2):
                        st.do(v.tensor_copy(TK[:, :, 64 * half:64 * half + 64], SM[:, :, 0:64]))
                    ts(wi[:, :, :], SM[:, :, 64:80], 1.0 / 32, None, ALU.mult)
                    st.settle()
                    rotate(TK[:, :, :].rearrange("p t (h d) -> p t h d", h=2)[:, :, :, 0:16], "cos_i", "sin_i", 2, 8)
                    dve.sem_inc(sem("ki_ready"), 1)
                elif kind in ("q", "kv", "qi"):
                    dve.wait_ge(sem("copied"), c - first["qi"] + 2)
                    if kind == "q":
                        rotate(T[:, :, :].rearrange("p t (h d) -> p t h d", h=4)[:, :, :, 0:32], "cos_a", "sin_a", 4, 16)
                    elif kind == "kv":
                        rotate(T[:, :, 0:256].rearrange("p t (h d) -> p t h d", h=2)[:, :, :, 0:32], "cos_a", "sin_a", 2, 16)
                    else:
                        rotate(T[:, :, :].rearrange("p t (h d) -> p t h d", h=8)[:, :, :, 0:16], "cos_i", "sin_i", 8, 8)
                    dve.sem_inc(sem("rope_ready"), 1)
                elif kind == "out":
                    if i == 0:
                        dve.wait_ge(x_landed, 32 * TT)
                    for tt in range(TT):
                        key = ("P", c, tt)
                        part = H[:, tt, i * 512:(i + 1) * 512]
                        stt(part, part, ALPHA, filled(dve, key)[:, :], ALU.mult, ALU.add, *freed(key))
                        st.settle()
                        st.do(v.bn_stats(bst[:, tt, i, :], part))
                elif kind in ("va", "q2", "k2"):
                    n = ("va", "q2", "k2").index(kind)
                    dve.wait_ge(sem("copied"), 7 + n)
                    if kind == "va":
                        tt_(SQ, VA, VA, ALU.mult)
                        st.settle()
                    sq = SQ[:, :, :].rearrange("p t (h d) -> p (t h) d", d=P)
                    st.do(v.tensor_reduce(ss[:, 0:16], sq, AX.X, ALU.add))
                    st.settle()
                    inv_mean(rs[:, 0:16], ss[:, 0:16], P, 1e-6, sem("mean_ready"))
                    dve.wait_ge(sem("root_ready"), n + 1)
                    buf = VA if kind == "va" else T2
                    x = buf[:, :, :].rearrange("p t (h d) -> p (t h) d", d=P)
                    tt_(x, x, per(rs[:, 0:16], [P, 16, P]), ALU.mult)
                    st.settle()
                    if kind == "va":
                        tt_(VA, VA, gmg[:, :].unsqueeze(1).to_broadcast([P, TT, 512]), ALU.mult)
                    else:
                        dve.sem_inc(sem("norm_ready"), 1)
                elif kind == "out2":
                    if i == 0:
                        dve.wait_ge(sem("gate_landed"), 32)
                    for tt in range(TT):
                        key = ("P", c, tt)
                        tt_(gtmp, filled(dve, key)[:, :], gate[:, i * 512:(i + 1) * 512], ALU.mult, *freed(key))
                        st.settle()
                        part = H[:, tt, i * 512:(i + 1) * 512]
                        tt_(part, part, gtmp, ALU.add, sem("part_ready"))
                        st.settle()

            def stage(n):
                for c in STAGES[n]:
                    if c in MODSUM:
                        mod_take(MODSUM[c])
                    if c == IX_AT:
                        index_sums()
                    if c == CUM_AT:
                        take_sums()
                    work(c)
                    if chunks[c][0] == "small":
                        time_steps()
                    if c == IX_AT:
                        choose()
                    mod_hook(c)

            stage(0)
            bar()

            dve.wait_ge(sem("cum_exp"), 1)

            def heads(x, n=64):
                return x.rearrange("p (h e) -> p h e", e=n)

            def middle(i):
                dve.wait_ge(sem("diff_exp"), i + 1)
                bk = filled(dve, ("G", i))
                st.do(v.tensor_tensor(Mt[:, i % 2], Dm[:, i % 2], bk[:, 0:P].unsqueeze(1).to_broadcast([P, SR, P]), ALU.mult), *freed(("G", i)))
                st.settle()
                dve.sem_inc(sem("decay_ready"), 1)

            def back(i):
                c, g = divmod(i, SG)
                cols = slice(g * 256, (g + 1) * 256)
                st.settle()
                bk = filled(dve, ("Y", i))
                dve.wait_ge(sem("skip_ready"), c + 1)
                skip = xs[:, c, cols]
                if c:
                    tt_(heads(t1), heads(bk[:, 256:512]), per(eac[:, c, 4 * g:4 * g + 4], [P, 4, 64]), ALU.mult)
                    tt_(skip, bk[:, 0:256], skip, ALU.add)
                    st.settle()
                    st.do(v.tensor_tensor(t1, skip, t1, ALU.add), *freed(("Y", i)))
                else:
                    tt_(t1, bk[:, 0:256], skip, ALU.add, *freed(("Y", i)))
                st.settle()
                z = Z[:, c, cols]
                tt_(z, z, t1, ALU.mult, sem("gate_done"))
                if i < 12:
                    hs = Hst[:, cols]
                    bs = filled(dve, ("ST", i))
                    if c == 0:
                        st.do(v.tensor_copy(hs, bs[:, 0:256]), *freed(("ST", i)))
                    else:
                        tt_(heads(hs), heads(hs), per(cdec[:, c, 4 * g:4 * g + 4], [P, 4, 64]), ALU.mult)
                        st.settle()
                        tt_(hs, hs, bs[:, 0:256], ALU.add, *freed(("ST", i)))
                    st.settle()
                    dve.sem_inc(sem("state_ready"), 1)

            for i in range(16):
                middle(i)
                if i:
                    back(i - 1)
            back(15)
            dve.wait_ge(sem("ms_summed"), 16)
            inv_mean(rs[:, 0:16], ss[:, 0:16], 256, 1e-5, sem("ms_ready"))
            dve.wait_ge(sem("ms_root"), 1)
            for i in range(16):
                c, g = divmod(i, SG)
                z = Z[:, c, g * 256:(g + 1) * 256]
                ts(z, z, rs[:, i:i + 1], None, ALU.mult, s=sem("gated_ready"))
            bar()
            stage(1)
            bar()

            def logits(k):
                i, g = GROUPS[k]
                nk = (i + 1) * P
                if k >= 2:
                    for kb in range(GROUPS[k - 2][0] + 1):
                        filled(dve, ("PT", *GROUPS[k - 2], kb))
                for r in range(4):
                    key = ("S", i, 4 * g + r)
                    bk = filled(dve, key)
                    st.do(v.tensor_tensor_reduce(out=Pb[k % 2][:, r, 0:nk], in0=bk[:, 0:nk], in1=BIAS[i], scale=float(DH) ** -0.5,
                                                 scalar=-3e38, op0=ALU.add, op1=ALU.max, accum_out=mx[:, k % 2, r:r + 1]), *freed(key))
                st.settle()
                ts(nm[:, k % 2, :], mx[:, k % 2, :], -1.0, None, ALU.mult, s=sem("max_ready"))

            def normalise(k):
                nk = (GROUPS[k][0] + 1) * P
                dve.wait_ge(sem("exp_done"), k + 1)
                st.do(v.reciprocal(rc[:, k % 2, :], sm[:, k % 2, :]))
                st.settle()
                p = Pb[k % 2][:, :, 0:nk]
                tt_(p, p, per(rc[:, k % 2, :], [P, 4, nk]), ALU.mult, sem("probs_ready"))

            def take(k):
                i, g = GROUPS[k]
                key = ("PV", i, g)
                bk = filled(dve, key)
                o = M[:, 4 * g:4 * g + 4, i * P:(i + 1) * P]
                tt_(o, o, bk[:, :].rearrange("p (r q) -> p r q", r=4), ALU.mult, *freed(key))

            logits(0)
            for k in range(len(GROUPS)):
                if k + 1 < len(GROUPS):
                    logits(k + 1)
                normalise(k)
                if k:
                    take(k - 1)
            take(len(GROUPS) - 1)
            bar()
            stage(2)
            bar()

            for tt in range(TT):
                st.do(v.bn_aggr(mv[:, tt, :], bst[:, tt, :, :].rearrange("p c s -> p (c s)")))
            st.settle()
            ts(rs[:, 0:4], mv[:, :, 1], 1e-5, None, ALU.add)
            st.settle()
            st.do(v.reciprocal(rs[:, 0:4], rs[:, 0:4]), sem("var_ready"))
            dve.wait_ge(sem("var_root"), 1)
            dve.wait_ge(sem("ln_landed"), 32)
            stt(mv[:, :, 0], mv[:, :, 0], -1.0, rs[:, 0:4], ALU.mult, ALU.mult, s=sem("shift_ready"))
            for tt in range(TT):
                row = H[:, tt, :]
                dve.wait_ge(sem("standard_row"), tt + 1)
                tt_(row, row, lng, ALU.mult)
                st.settle()
                tt_(row, row, lnb, ALU.add, sem("h_rows"))
            stt(G1[:, :], MV[:, 1, :], 1.0, n1g[:, :], ALU.add, ALU.mult)
            st.settle()

            def norm_hidden(n):
                inv_mean(rs[:, 0:4], ss[:, 0:4], D, 1e-6, sem("msq_ready"))
                dve.wait_ge(sem("msq_root"), n + 1)
                for tt in range(TT // 2):
                    ts(XN[:, tt, :], H[:, tt, :], rs[:, tt:tt + 1], None, ALU.mult, s=sem("xn_ready"))

            dve.wait_ge(sem("squares_done"), 1)
            norm_hidden(0)
            dve.wait_ge(sem("ys_cleared"), 16)
            for kt in range(0, KD, 2):
                key = ("hT", kt)
                ts(X[:, kt, :], filled(dve, key)[:, :], G1[:, kt:kt + 1], MV[:, 0, kt:kt + 1], ALU.mult, ALU.add, *freed(key))
            bk = filled(dve, "wsT")
            tt_(WS[:, :, :], bk[:, :].rearrange("p (g t) -> p g t", g=4), C["upto"].unsqueeze(1).to_broadcast([P, 4, P]), ALU.mult, *freed("wsT"))
            bar()
            stage(3)
            bar()

            for tt in range(TT):
                key = ("SPG", tt)
                bk = filled(dve, key)
                for g in range(4):
                    cols = slice(g * P, (g + 1) * P)
                    stt(Y[:, tt, cols], bk[:, cols], pack[:, 98 + g:99 + g], UA[:, tt, cols], ALU.add, ALU.mult,
                        *(freed(key) if g == 3 else (None, None)))
            def negative_abs(h):
                if h >= 2:
                    dve.wait_ge(sem("log_a_ready"), 4 * (h - 1))
                for j in range(4):
                    z = filled(dve, ("Z", h, j))[:, 0:S - P * j]
                    ts(tri(SPall[h % 2], j), z, 0.0, None, ALU.max)
                st.settle()
                for j in range(4):
                    z = ps[use["Z", h, j][0]][:, 0:S - P * j]
                    stt(tri(EAall[h % 2], j), tri(SPall[h % 2], j), -2.0, z, ALU.mult, ALU.add)
                st.settle()
                dve.sem_inc(sem("abs_ready"), 1)

            def softplus(h):
                dve.wait_ge(sem("log_ready"), h + 1)
                tt_(SPall[h % 2], SPall[h % 2], EAall[h % 2], ALU.add)
                st.settle()
                for j in range(4):
                    part = tri(SPall[h % 2], j)[:, 0:P]
                    tt_(part, part, C["before"], ALU.mult)
                st.settle()
                dve.sem_inc(sem("fail_ready"), 1)

            def take_values(h):
                key = ("O", h)
                bk = filled(dve, key)
                st.do(v.tensor_copy(Y[:, :, 512 + h * P:512 + (h + 1) * P], bk[:, :].rearrange("p (t d) -> p t d", t=TT)), *freed(key))

            negative_abs(0)
            negative_abs(1)
            for h in (0, 2):
                softplus(h)
                softplus(h + 1)
                for hh in (h, h + 1):
                    take_values(hh)
                    if h == 0:
                        negative_abs(hh + 2)
            st.settle()
            tt_(YSQ, Y, Y, ALU.mult)
            st.settle()
            st.do(v.tensor_reduce(ss[:, 0:32], YSQ[:, :, :].rearrange("p t (h d) -> p (t h) d", d=P), AX.X, ALU.add))
            st.settle()
            inv_mean(rs[:, 0:32], ss[:, 0:32], P, 1e-6, sem("mean_ready"))
            dve.wait_ge(sem("root_ready"), 4)
            x = Y[:, :, :].rearrange("p t (h d) -> p (t h) d", d=P)
            tt_(x, x, per(rs[:, 0:32], [P, 32, P]), ALU.mult, sem("y_ready"))
            bar()
            stage(4)
            bar()
            stt(G2[:, :], MV[:, 4, :], 1.0, n2g[:, :], ALU.add, ALU.mult)
            st.settle()
            dve.wait_ge(sem("part_squared"), 16)
            st.do(v.tensor_reduce(ss[:, 16:20], ss[:, 0:16].rearrange("p (t i) -> p t i", t=TT), AX.X, ALU.add))
            st.settle()
            st.do(v.tensor_copy(ss[:, 0:4], ss[:, 16:20]))
            st.settle()
            norm_hidden(1)
            for kt in range(0, KD, 2):
                key = ("h2T", kt)
                ts(X[:, kt, :], filled(dve, key)[:, :], G2[:, kt:kt + 1], MV[:, 3, kt:kt + 1], ALU.mult, ALU.add, *freed(key))
            st.settle()
            dve.sem_inc(sem("h2T_dve"), 8)

            bk = filled(dve, "router")
            tt_(L[:, :, :], bk[:, 0:144].rearrange("p (t e) -> p t e", t=TT), br[:, :].unsqueeze(1).to_broadcast([P, TT, 36]), ALU.add, *freed("router"))
            st.settle()
            gl = L[:, :, 0:4]
            st.do(v.tensor_reduce(gm1[:, :], gl, AX.X, ALU.max))
            st.settle()
            tt_(r4[:, :, :], gl, per(gm1[:, :], [P, TT, 4]), ALU.subtract)
            tt_(oh[:, :, :], gl, per(gm1[:, :], [P, TT, 4]), ALU.is_equal, sem("group_in"))

            def first_of(onehot, scratch_max, width):
                rank = C["rank4" if width == 4 else "rank8"].unsqueeze(1).to_broadcast([P, TT, width])
                st.settle()
                tt_(onehot, onehot, rank, ALU.mult)
                st.settle()
                st.do(v.tensor_reduce(scratch_max, onehot, AX.X, ALU.max))
                st.settle()
                tt_(onehot, onehot, per(scratch_max, [P, TT, width]), ALU.is_equal)
                st.settle()

            first_of(oh[:, :, :], tmx[:, :], 4)
            dve.wait_ge(sem("group_exp"), 1)
            st.do(v.tensor_reduce(pg[:, :], r4[:, :, :], AX.X, ALU.add))
            st.settle()
            st.do(v.reciprocal(pg[:, :], pg[:, :]))
            for g in range(NG):
                tt_(el3[:, :, g, :], L[:, :, 4 + 8 * g:12 + 8 * g], oh[:, :, g:g + 1].to_broadcast([P, TT, 8]), ALU.mult)
            st.settle()
            st.do(v.tensor_reduce(el[:, :, :], el3[:, :, :, :].rearrange("p t g j -> p t j g"), AX.X, ALU.add))
            st.settle()
            st.do(v.tensor_reduce(e1v[:, :], el[:, :, :], AX.X, ALU.max))
            st.settle()
            tt_(o1[:, :, :], el[:, :, :], per(e1v[:, :], [P, TT, 8]), ALU.is_equal)
            first_of(o1[:, :, :], tmx[:, :], 8)
            stt(el[:, :, :], o1[:, :, :], OUT_OF_REACH, el[:, :, :], ALU.mult, ALU.add)
            st.settle()
            st.do(v.tensor_reduce(e2v[:, :], el[:, :, :], AX.X, ALU.max))
            st.settle()
            tt_(o2[:, :, :], el[:, :, :], per(e2v[:, :], [P, TT, 8]), ALU.is_equal)
            first_of(o2[:, :, :], tmx[:, :], 8)
            tt_(e2v[:, :], e2v[:, :], e1v[:, :], ALU.subtract, sem("pair_in"))
            for E, o in ((E1, o1), (E2, o2)):
                for g in range(NG):
                    tt_(E[:, :, 8 * g:8 * g + 8], o[:, :, :], oh[:, :, g:g + 1].to_broadcast([P, TT, 8]), ALU.mult)
            st.settle()
            tt_(EM[:, :, :], E1[:, :, :], E2[:, :, :], ALU.add, sem("choice_ready"))
            dve.wait_ge(sem("pair_exp"), 1)
            ts(wa[:, :], e2v[:, :], 1.0, None, ALU.add)
            st.settle()
            st.do(v.reciprocal(wa[:, :], wa[:, :]))
            st.settle()
            tt_(wa[:, :], wa[:, :], pg[:, :], ALU.mult)
            st.settle()
            tt_(wb[:, :], wa[:, :], e2v[:, :], ALU.mult)
            bk = filled(dve, "rank")
            cnt = RA[:, 0:256].rearrange("p (e k) -> p e k", k=8)
            st.do(v.tensor_copy(nbk[:, :], bk[:, P:P + NE]))
            st.settle()
            tt_(cnt, per(nbk[:, :], [P, NE, 8]), C["thresholds"].unsqueeze(1).to_broadcast([P, NE, 8]), ALU.is_gt)
            st.settle()
            st.do(v.tensor_reduce(nbk[:, :], cnt, AX.X, ALU.add))
            st.settle()
            st.do(v.tensor_tensor_scan(bend[:, :], C["ones"][:, 0:NE], nbk[:, :], 0.0, ALU.mult, ALU.add))
            st.settle()
            tt_(nbk[:, :], bend[:, :], nbk[:, :], ALU.subtract)
            st.settle()
            stt(slot[:, :, :], nbk[:, :].unsqueeze(1).to_broadcast([P, TT, NE]), float(BLK), bk[:, 0:P].rearrange("p (t e) -> p t e", t=TT),
                ALU.mult, ALU.add, *freed("rank"))
            st.settle()
            for k, E in enumerate((E1, E2)):
                tt_(E[:, :, :], E[:, :, :], slot[:, :, :], ALU.mult)
                st.settle()
                st.do(v.tensor_reduce(sl[:, k, :], E[:, :, :], AX.X, ALU.add))
            st.settle()
            st.do(v.tensor_copy(sli[:, :, :], sl[:, :, :]))
            st.do(v.tensor_copy(toki[:, :], C["tokens"]))
            wide = RA[0:1, 256:256 + NBLK * NE].rearrange("p (b e) -> p b e", e=NE)
            tt_(wide, bend[0:1, :].unsqueeze(1).to_broadcast([1, NBLK, NE]), per(C["block_no"][0:1, :], [1, NBLK, NE]), ALU.is_le)
            st.settle()
            st.do(v.tensor_reduce(blke[:, :], wide, AX.X, ALU.add))
            st.settle()
            ts(blke[:, :], blke[:, :], NE - 1.0, None, ALU.min)
            st.settle()
            st.do(v.tensor_copy(blki[:, :], blke[:, :]))
            st.do(v.tensor_copy(nbi[:, :], bend[0:1, NE - 1:NE]))
            st.settle()
            dve.sem_inc(sem("routed"), 1)
            bar()
            blocks = dve.value_load(nbi[0:1, 0:1], min_val=1, max_val=NBLK)
            for name in ("t_taken", "h_ready", "y_taken_dve"):
                dve.sem_inc(sem(name), 1)

            def take_turned(block, w, before):
                dve.wait_ge(sem(f"t_done{w}"), before + 2)
                dve.wait_ge(sem(f"up_done{w}"), before + 1)
                for n in range(2):
                    half = slice(8 * n, 8 * n + 8)
                    ins = v.tensor_tensor(xmul[:, half, :], ps[n][:, :].rearrange("p (k s) -> p k s", s=BLK),
                                          per(G2[:, half], [P, 8, BLK]), ALU.mult)
                ins.then_inc(sem("t_taken"), 1)
                dve.wait_ge(sem("t_taken"), block + 2)
                v.tensor_tensor(xgT[w], xmul, per(MV[:, 3, :], [P, KD, BLK]), ALU.add).then_inc(sem("xt_ready"), 1)

            take_turned(0, 0, 0)
            with dve.Fori(0, NBLK // 2) as i:
                with dve.If(i * 2 < blocks):
                    for u in range(2):
                        dve.wait_ge(sem("silu_gate"), i * 2 + u + 1)
                        v.tensor_tensor(hb[u], SGt[u].rearrange("p (m s) -> p m s", m=2), ps[3][:, 0:P].rearrange("p (m s) -> p m s", m=2),
                                        ALU.mult).then_inc(sem("h_ready"), 1)
                        take_turned(i * 2 + u + 1, 1 - u, i + u)
                        dve.wait_ge(sem(f"down_done{u}"), i + 2)
                        dve.wait_ge(sem(f"y_stored{u}"), i * 16 + 16)
                        for n in range(4):
                            part = slice(n * 512, (n + 1) * 512)
                            ins = v.tensor_tensor(yb[u][:, part], ps[4 + n][0:BLK, :], gate2[0:BLK, part], ALU.mult)
                        ins.then_inc(sem("y_taken_dve"), 1)
            dve.sem_inc(phase["dve"], 1)
            for tt in range(TT):
                y0, y1 = picked[tt % 2]
                dve.wait_ge(sem(f"picked_landed{tt % 2}"), 32 * (tt // 2 + 1))
                row = H[:, tt, :]
                stt(row, y0, wa[:, tt:tt + 1], row, ALU.mult, ALU.add)
                st.settle()
                stt(row, y1, wb[:, tt:tt + 1], row, ALU.mult, ALU.add, s=sem("out_ready"))
                st.settle()
                dve.sem_inc(sem("picked_used"), 1)


_INS = ["x", "w_in", "w_out", "conv_w", "conv_b", "dt_bias", "a_log", "d_skip", "ssd_norm_w", "ln_g", "ln_b", "c_2",
        "w_mod_2", "b_mod_2", "mod_layer_2", "norm1_g_2", "w_in_2", "gm_norm_g_2", "gm_ws_2", "gm_bs_2", "q_norm_g_2",
        "k_norm_g_2", "out_norm_g_2", "w_out_2", "norm2_g_2", "w_group_2", "b_group_2", "w_route_2", "b_route_2",
        "w_gate_2", "w_up_2", "w_down_2"]


def kernel(**inputs):
    import concourse.bacc as bacc
    from concourse.bass_utils import run_bass_kernel_spmd as run

    nc = bacc.Bacc("TRN2", target_bir_lowering=False, num_devices=1)
    arrays, args = {}, {}
    for name in _INS:
        arr = np.ascontiguousarray(inputs[name])
        arrays[f"in_{name}"] = arr
        args[name] = nc.dram_tensor(f"in_{name}", arr.shape, mybir.dt.from_np(arr.dtype), kind="ExternalInput").ap()
    arrays["in_const"] = CONST
    args["const"] = nc.dram_tensor("in_const", CONST.shape, F32, kind="ExternalInput").ap()
    out = nc.dram_tensor("out_0", (1, S, D), F32, kind="ExternalOutput").ap()
    program(nc, args, out)
    r = run(nc, [arrays], core_ids=[0])
    return r.results[0]["out_0"]
```
